# Optimizing a Trainium2 kernel written in Bass

```python
import jax, jax.numpy as jnp
from jax import lax
import numpy as np

'''One inference step of a hybrid decoder layer stack (parallel gated branches):
  mixer A = causal multi-scale pooling mixer (PoolFormer style, windows 2/4/8/16),
  mixer B = forgetting attention (FoX) with QK-norm, no positional encoding,
  channel mixer = PEER product-key single-neuron expert retrieval.
Two request groups share all weights:
  prompt: x_prompt (BATCH, SEQ, D_MODEL), positions 0..SEQ-1
  sample: x_sample (DEC_BATCH, DEC_SEQ, D_MODEL), positions PAST_LEN..PAST_LEN+DEC_SEQ-1,
          reading a paged K/V/log-forget cache through page_table (DEC_BATCH, N_PAGES)
          and a per-sequence pooling history buffer.
State inputs:
  cache_k, cache_v : (DEPTH, N_PHYS, PAGE_SIZE, N_HEADS, HEAD_DIM)  paged (QK-normed keys, values)
  cache_logf       : (DEPTH, N_PHYS, PAGE_SIZE, N_HEADS)            paged log forget gates
  state_pool       : (DEPTH, DEC_BATCH, POOL_HIST, D_POOL)          last 15 pooling-input rows
Returns the tuple
  (y_prompt (BATCH, SEQ, D_MODEL), y_sample (DEC_BATCH, DEC_SEQ, D_MODEL),
   k_prompt (DEPTH, BATCH, SEQ, N_HEADS, HEAD_DIM), v_prompt (same),
   logf_prompt (DEPTH, BATCH, SEQ, N_HEADS), pool_prompt (DEPTH, BATCH, POOL_HIST, D_POOL),
   k_sample (DEPTH, DEC_BATCH, DEC_SEQ, N_HEADS, HEAD_DIM), v_sample (same),
   logf_sample (DEPTH, DEC_BATCH, DEC_SEQ, N_HEADS), pool_sample (DEPTH, DEC_BATCH, POOL_HIST, D_MODEL//2))
'''

D_MODEL = 1024
BATCH = 1
SEQ = 1024
DEPTH = 1
DEC_BATCH = 8
DEC_SEQ = 8
PAST_LEN = 512
PAGE_SIZE = 128

D_POOL = D_MODEL // 2
POOL_WINDOWS = (2, 4, 8, 16)
POOL_GROUPS = len(POOL_WINDOWS)
POOL_GC = D_POOL // POOL_GROUPS
POOL_HIST = max(POOL_WINDOWS) - 1
D_ATTN = D_MODEL // 2
HEAD_DIM = 64
N_HEADS = D_ATTN // HEAD_DIM
Q_BLOCK = 128
ATTN_SCALE = HEAD_DIM ** -0.5
N_KEYS = 128
N_EXPERTS = N_KEYS * N_KEYS
PEER_HEADS = 8
PEER_TOPK = 16
D_KEY = 256
D_KEY_HALF = D_KEY // 2
PEER_CHUNK = 128
RMS_EPS = 1e-6
D_IN = D_POOL + 3 * D_ATTN + N_HEADS + 2 * D_MODEL
SPLITS = (D_POOL, D_POOL + D_ATTN, D_POOL + 2 * D_ATTN, D_POOL + 3 * D_ATTN,
          D_POOL + 3 * D_ATTN + N_HEADS, D_POOL + 3 * D_ATTN + N_HEADS + D_MODEL)

kernel_name = 'hybrid_pool_fox_peer_decode_step'

def rmsnorm(x, g):
    xf = x.astype(jnp.float32)
    ms = jnp.mean(xf * xf, axis=-1, keepdims=True)
    return (xf * lax.rsqrt(ms + RMS_EPS) * g.astype(jnp.float32)).astype(x.dtype)

def project_in(x, norm_mix_g, w_in, b_forget, q_norm_g, k_norm_g):
    B, L, _ = x.shape
    xn = rmsnorm(x, norm_mix_g)
    p = xn @ w_in
    u_pool, q, k, v, f_logit, gate_a, gate_b = jnp.split(p, SPLITS, axis=-1)
    q = rmsnorm(q.reshape(B, L, N_HEADS, HEAD_DIM), q_norm_g)
    k = rmsnorm(k.reshape(B, L, N_HEADS, HEAD_DIM), k_norm_g)
    v = v.reshape(B, L, N_HEADS, HEAD_DIM)
    logf = jax.nn.log_sigmoid((f_logit + b_forget).astype(jnp.float32))
    return u_pool, q, k, v, logf, gate_a, gate_b

def pool_mixer(u, hist, pos0, pool_mix_w, pool_scale):
    B, L, _ = u.shape
    u_ext = jnp.concatenate([hist.astype(u.dtype), u], axis=1)
    c = jnp.cumsum(u_ext.astype(jnp.float32), axis=1)
    c = jnp.concatenate([jnp.zeros((B, 1, D_POOL), jnp.float32), c], axis=1)
    pos = pos0 + jnp.arange(L)
    start = POOL_HIST + 1
    outs = []
    for gi, w in enumerate(POOL_WINDOWS):
        sl = slice(gi * POOL_GC, (gi + 1) * POOL_GC)
        wsum = c[:, start:start + L, sl] - c[:, start - w:start - w + L, sl]
        cnt = jnp.minimum(pos + 1, w).astype(jnp.float32)
        outs.append(wsum / cnt[None, :, None] - u[..., sl].astype(jnp.float32))
    m = jnp.stack(outs, axis=2)
    m = jnp.einsum('blgc,gcd->blgd', m, pool_mix_w.astype(jnp.float32)).reshape(B, L, D_POOL)
    out = (m * pool_scale).astype(u.dtype)
    return out, u_ext[:, -POOL_HIST:]

def attend(q, k, v, cq, ck, qpos, kpos):
    logits = jnp.einsum('bqhd,bkhd->bhqk', q.astype(jnp.float32), k.astype(jnp.float32)) * ATTN_SCALE
    bias = jnp.transpose(cq, (0, 2, 1))[..., :, None] - jnp.transpose(ck, (0, 2, 1))[..., None, :]
    mask = kpos[None, :] <= qpos[:, None]
    logits = jnp.where(mask, logits + bias, -jnp.inf)
    p = jax.nn.softmax(logits, axis=-1)
    o = jnp.einsum('bhqk,bkhd->bqhd', p, v.astype(jnp.float32))
    return o.astype(v.dtype)

def prompt_attention(q, k, v, logf):
    B, S = q.shape[:2]
    c = jnp.cumsum(logf.astype(jnp.float32), axis=1)
    kpos = jnp.arange(S)

    def block(i):
        s0 = i * Q_BLOCK
        qb = lax.dynamic_slice_in_dim(q, s0, Q_BLOCK, axis=1)
        cqb = lax.dynamic_slice_in_dim(c, s0, Q_BLOCK, axis=1)
        return attend(qb, k, v, cqb, c, s0 + jnp.arange(Q_BLOCK), kpos)

    o = lax.map(block, jnp.arange(S // Q_BLOCK))
    return jnp.transpose(o, (1, 0, 2, 3, 4)).reshape(B, S, D_ATTN)

def sample_attention(q, k, v, logf, cache_k, cache_v, cache_logf, page_table):
    DB, T = q.shape[:2]
    n_pages = page_table.shape[1]
    P = n_pages * PAGE_SIZE
    k_past = cache_k[page_table].reshape(DB, P, N_HEADS, HEAD_DIM)
    v_past = cache_v[page_table].reshape(DB, P, N_HEADS, HEAD_DIM)
    lf_past = cache_logf[page_table].reshape(DB, P, N_HEADS)
    k_all = jnp.concatenate([k_past, k.astype(k_past.dtype)], axis=1)
    v_all = jnp.concatenate([v_past, v.astype(v_past.dtype)], axis=1)
    c_all = jnp.cumsum(jnp.concatenate([lf_past.astype(jnp.float32), logf], axis=1), axis=1)
    o = attend(q, k_all, v_all, c_all[:, P:], c_all, P + jnp.arange(T), jnp.arange(P + T))
    return o.reshape(DB, T, D_ATTN)

def peer_chunk(xc, w_query, sub_keys, peer_u, peer_v):
    C = xc.shape[0]
    q = (xc @ w_query).reshape(C, PEER_HEADS, 2, D_KEY_HALF)
    s = jnp.einsum('chpd,hpnd->chpn', q.astype(jnp.float32), sub_keys.astype(jnp.float32))
    s1, i1 = lax.top_k(s[:, :, 0], PEER_TOPK)
    s2, i2 = lax.top_k(s[:, :, 1], PEER_TOPK)
    cand_s = (s1[..., :, None] + s2[..., None, :]).reshape(C, PEER_HEADS, PEER_TOPK * PEER_TOPK)
    cand_i = (i1[..., :, None] * N_KEYS + i2[..., None, :]).reshape(C, PEER_HEADS, PEER_TOPK * PEER_TOPK)
    top_s, top_pos = lax.top_k(cand_s, PEER_TOPK)
    idx = jnp.take_along_axis(cand_i, top_pos, axis=-1)
    g = jax.nn.softmax(top_s, axis=-1)
    u = peer_u[idx]
    a = jax.nn.gelu(jnp.einsum('cd,chkd->chk', xc, u).astype(jnp.float32), approximate=False)
    v = peer_v[idx]
    return jnp.einsum('chk,chkd->cd', (g * a).astype(v.dtype), v).astype(xc.dtype)

def peer_ffn(xn, w_query, sub_keys, peer_u, peer_v):
    n = xn.shape[0]
    pad = (-n) % PEER_CHUNK
    xp = jnp.pad(xn, ((0, pad), (0, 0))).reshape(-1, PEER_CHUNK, D_MODEL)
    out = lax.map(lambda xc: peer_chunk(xc, w_query, sub_keys, peer_u, peer_v), xp)
    return out.reshape(-1, D_MODEL)[:n]

def merge_and_ffn(x, pool_out, attn_out, gate_a, gate_b, w_branch_pool, w_branch_attn, w_out,
                  norm_ffn_g, w_query, sub_keys, peer_u, peer_v):
    mixed = jax.nn.sigmoid(gate_a) * (pool_out @ w_branch_pool) + jax.nn.sigmoid(gate_b) * (attn_out @ w_branch_attn)
    h = x + mixed @ w_out
    hn = rmsnorm(h, norm_ffn_g)
    return h + peer_ffn(hn.reshape(-1, D_MODEL), w_query, sub_keys, peer_u, peer_v).reshape(h.shape)

def layer_step(x_p, x_s, cache_k, cache_v, cache_logf, state_pool, page_table, norm_mix_g, w_in, b_forget,
               q_norm_g, k_norm_g, pool_mix_w, pool_scale, w_branch_pool, w_branch_attn, w_out, norm_ffn_g,
               w_query, sub_keys, peer_u, peer_v):
    u_p, q_p, k_p, v_p, lf_p, ga_p, gb_p = project_in(x_p, norm_mix_g, w_in, b_forget, q_norm_g, k_norm_g)
    hist0 = jnp.zeros((x_p.shape[0], POOL_HIST, D_POOL), u_p.dtype)
    pool_p, hist_p = pool_mixer(u_p, hist0, 0, pool_mix_w, pool_scale)
    attn_p = prompt_attention(q_p, k_p, v_p, lf_p)
    y_p = merge_and_ffn(x_p, pool_p, attn_p, ga_p, gb_p, w_branch_pool, w_branch_attn, w_out,
                        norm_ffn_g, w_query, sub_keys, peer_u, peer_v)
    u_s, q_s, k_s, v_s, lf_s, ga_s, gb_s = project_in(x_s, norm_mix_g, w_in, b_forget, q_norm_g, k_norm_g)
    pool_s, hist_s = pool_mixer(u_s, state_pool, PAST_LEN, pool_mix_w, pool_scale)
    attn_s = sample_attention(q_s, k_s, v_s, lf_s, cache_k, cache_v, cache_logf, page_table)
    y_s = merge_and_ffn(x_s, pool_s, attn_s, ga_s, gb_s, w_branch_pool, w_branch_attn, w_out,
                        norm_ffn_g, w_query, sub_keys, peer_u, peer_v)
    return y_p, y_s, k_p, v_p, lf_p, hist_p, k_s, v_s, lf_s, hist_s

def setup_inputs(seed: int = 0) -> dict:
    key = jax.random.key(seed)
    ks = jax.random.split(key, 24)
    nrm = jax.random.normal
    n_pages = PAST_LEN // PAGE_SIZE
    n_used = DEC_BATCH * n_pages
    n_phys = n_used + (n_used + 3) // 4
    page_table = jax.random.permutation(ks[0], n_phys)[:n_used].reshape(DEC_BATCH, n_pages).astype(jnp.int32)
    L = DEPTH
    return {
        'x_prompt': nrm(ks[1], (BATCH, SEQ, D_MODEL), jnp.float32),
        'x_sample': nrm(ks[2], (DEC_BATCH, DEC_SEQ, D_MODEL), jnp.float32),
        'cache_k': nrm(ks[3], (L, n_phys, PAGE_SIZE, N_HEADS, HEAD_DIM), jnp.float32),
        'cache_v': nrm(ks[4], (L, n_phys, PAGE_SIZE, N_HEADS, HEAD_DIM), jnp.float32),
        'cache_logf': jax.nn.log_sigmoid(3.0 + nrm(ks[5], (L, n_phys, PAGE_SIZE, N_HEADS), jnp.float32)),
        'state_pool': nrm(ks[6], (L, DEC_BATCH, POOL_HIST, D_POOL), jnp.float32),
        'page_table': page_table,
        'norm_mix_g': 1.0 + 0.02 * nrm(ks[7], (L, D_MODEL), jnp.float32),
        'w_in': nrm(ks[8], (L, D_MODEL, D_IN), jnp.float32) * D_MODEL ** -0.5,
        'b_forget': 3.0 + 0.5 * nrm(ks[9], (L, N_HEADS), jnp.float32),
        'q_norm_g': 1.0 + 0.02 * nrm(ks[10], (L, HEAD_DIM), jnp.float32),
        'k_norm_g': 1.0 + 0.02 * nrm(ks[11], (L, HEAD_DIM), jnp.float32),
        'pool_mix_w': nrm(ks[12], (L, POOL_GROUPS, POOL_GC, POOL_GC), jnp.float32) * POOL_GC ** -0.5,
        'pool_scale': 1.0 + 0.05 * nrm(ks[13], (L, D_POOL), jnp.float32),
        'w_branch_pool': nrm(ks[14], (L, D_POOL, D_MODEL), jnp.float32) * D_POOL ** -0.5,
        'w_branch_attn': nrm(ks[15], (L, D_ATTN, D_MODEL), jnp.float32) * D_ATTN ** -0.5,
        'w_out': nrm(ks[16], (L, D_MODEL, D_MODEL), jnp.float32) * D_MODEL ** -0.5,
        'norm_ffn_g': 1.0 + 0.02 * nrm(ks[17], (L, D_MODEL), jnp.float32),
        'w_query': nrm(ks[18], (L, D_MODEL, PEER_HEADS * D_KEY), jnp.float32) * D_MODEL ** -0.5,
        'sub_keys': nrm(ks[19], (L, PEER_HEADS, 2, N_KEYS, D_KEY_HALF), jnp.float32) * D_KEY_HALF ** -0.5,
        'peer_u': nrm(ks[20], (L, N_EXPERTS, D_MODEL), jnp.float32) * D_MODEL ** -0.5,
        'peer_v': nrm(ks[21], (L, N_EXPERTS, D_MODEL), jnp.float32) * (0.5 * PEER_HEADS ** -0.5),
    }

def reference(x_prompt, x_sample, cache_k, cache_v, cache_logf, state_pool, page_table, norm_mix_g, w_in,
              b_forget, q_norm_g, k_norm_g, pool_mix_w, pool_scale, w_branch_pool, w_branch_attn, w_out,
              norm_ffn_g, w_query, sub_keys, peer_u, peer_v):
    x_p, x_s = x_prompt, x_sample
    kp_l, vp_l, lfp_l, pp_l, ks_l, vs_l, lfs_l, ps_l = [], [], [], [], [], [], [], []
    for l in range(DEPTH):
        x_p, x_s, k_p, v_p, lf_p, h_p, k_s, v_s, lf_s, h_s = layer_step(
            x_p, x_s, cache_k[l], cache_v[l], cache_logf[l], state_pool[l], page_table,
            norm_mix_g[l], w_in[l], b_forget[l], q_norm_g[l], k_norm_g[l], pool_mix_w[l], pool_scale[l],
            w_branch_pool[l], w_branch_attn[l], w_out[l], norm_ffn_g[l], w_query[l], sub_keys[l],
            peer_u[l], peer_v[l])
        kp_l.append(k_p); vp_l.append(v_p); lfp_l.append(lf_p); pp_l.append(h_p)
        ks_l.append(k_s); vs_l.append(v_s); lfs_l.append(lf_s); ps_l.append(h_s)
    k_prompt = jnp.stack(kp_l); v_prompt = jnp.stack(vp_l)
    logf_prompt = jnp.stack(lfp_l); pool_prompt = jnp.stack(pp_l)
    k_sample = jnp.stack(ks_l); v_sample = jnp.stack(vs_l)
    logf_sample = jnp.stack(lfs_l); pool_sample = jnp.stack(ps_l)
    return (x_p, x_s, k_prompt, v_prompt, logf_prompt, pool_prompt, k_sample, v_sample, logf_sample, pool_sample)


_drawn_inputs = setup_inputs


def setup_inputs(seed=0):
    import zlib

    import numpy as np

    out = dict(_drawn_inputs(seed))
    spreads = {}
    factors = {'norm_mix_g': 2.838, 'q_norm_g': 8.0, 'k_norm_g': 2.741, 'norm_ffn_g': 4.72}
    for name, (base, spread) in spreads.items():
        noise = np.random.default_rng([zlib.crc32(name.encode()), seed]).standard_normal(out[name].shape)
        drawn = base * np.exp(spread * noise) if base else spread * noise
        out[name] = __import__('jax').numpy.asarray(drawn.astype(out[name].dtype))
    for name, factor in factors.items():
        out[name] = (out[name] * factor).astype(out[name].dtype)
    return out
```

```python
from contextlib import ExitStack

import concourse.bass as bass
from concourse import mybir

F32 = mybir.dt.float32
BF16 = mybir.dt.bfloat16
U32 = mybir.dt.uint32
I32 = mybir.dt.int32
ALU = mybir.AluOpType
ACT = mybir.ActivationFunctionType
AX = mybir.AxisListType
ds = bass.ds

P = 128
EPS = 1e-6
NEG = -1.0e30
LOWEST = -3.0e38
POOL_WINDOWS = (2, 4, 8, 16)


def build(nc, x_prompt, x_sample, cache_k, cache_v, cache_logf, state_pool, page_table, norm_mix_g, w_in,
          b_forget, q_norm_g, k_norm_g, pool_mix_w, pool_scale, w_branch_pool, w_branch_attn, w_out,
          norm_ffn_g, w_query, sub_keys, peer_u, peer_v,
          y_prompt, y_sample, k_prompt, v_prompt, logf_prompt, pool_prompt,
          k_sample, v_sample, logf_sample, pool_sample):
    _, SEQ, D = x_prompt.shape
    NSEQ, DSEQ, _ = x_sample.shape
    _, NPHYS, PAGE, H, DH = cache_k.shape
    NPAGES = page_table.shape[1]
    HIST = state_pool.shape[2]
    DA = H * DH
    DP = state_pool.shape[3]
    KD = D // P
    NG = DP // P
    TS = NSEQ * DSEQ
    T = SEQ + TS
    NT = SEQ // P
    PAST = NPAGES * PAGE
    ALLK = PAST + DSEQ
    PH = sub_keys.shape[1]
    NK = sub_keys.shape[3]
    TOPK = 16
    NPICK = PH * TOPK
    NPC = PH * 2
    SCALE = float(DH) ** -0.5
    INV = 1.0 / SCALE
    COLS = [(0, 512), (512, 512), (SEQ, TS)]
    QKV0 = DP
    F0 = DP + 3 * DA
    GA0 = F0 + H
    GB0 = GA0 + D
    assert P == PAGE and DH * 2 == P and PAST == 512 and SEQ == 1024 and NK == P

    xp = x_prompt.rearrange("a t d -> (a t) d")
    xs_dram = x_sample.rearrange("b t d -> (b t) d")
    kp_out = k_prompt.rearrange("l a t h d -> (l a t) (h d)")
    vp_out = v_prompt.rearrange("l a t h d -> (l a t) (h d)")
    ks_out = k_sample.rearrange("l b t h d -> (l b t) (h d)")
    vs_out = v_sample.rearrange("l b t h d -> (l b t) (h d)")
    lfp_out = logf_prompt.rearrange("l a (n p) h -> p (l a n) h", p=P)
    lfs_out = logf_sample.rearrange("l b t h -> (l b t) h")
    yp_out = y_prompt.rearrange("a t d -> (a t) d")
    ys_out = y_sample.rearrange("b t d -> (b t) d")
    win = w_in[0].rearrange("(c p) n -> p c n", p=P)
    ck = cache_k[0].rearrange("n t h d -> n t (h d)")
    cv = cache_v[0].rearrange("n t h d -> n t (h d)")
    clf = cache_logf[0]
    h_dram = nc.dram_tensor("h_scratch", [T, D], F32, kind="Internal").ap()
    hn_dram = nc.dram_tensor("hn_scratch", [T, D], F32, kind="Internal").ap()

    with ExitStack() as top:
        def sb(ctx, name, shape, dt=F32):
            return ctx.enter_context(nc.sbuf_tensor(name, shape, dt))

        def ps(ctx, name, shape, dt=F32):
            return ctx.enter_context(nc.psum_tensor(name, shape, dt))

        in_use, spare = [], []

        def sem(name):
            if spare:
                return spare.pop(0)
            in_use.append(top.enter_context(nc.semaphore(name)))
            return in_use[-1]

        ident = sb(top, "ident", [P, P])
        identb = sb(top, "identb", [P, P], BF16)

        causal = sb(top, "causal", [P, P], BF16)
        causal8 = sb(top, "causal8", [DSEQ, DSEQ], BF16)
        rep_q = sb(top, "rep_q", [DSEQ, H, DSEQ], BF16)
        same_head = sb(top, "same_head", [H, H, DSEQ])
        rcnt = sb(top, "rcnt", [P, 16])
        eps_col = sb(top, "eps_col", [P, 1])

        c_set, c_sel, c_dve, c_iota = sem("c_set"), sem("c_sel"), sem("c_dve"), sem("c_iota")
        with nc.Block() as block:
            @block.gpsimd
            def _(pool):
                pool.memset(ident[:], 0.0).then_inc(c_set, 1)
                pool.memset(identb[:], 0.0).then_inc(c_set, 1)
                pool.memset(causal[:], 0.0).then_inc(c_set, 1)
                pool.memset(causal8[:], 0.0).then_inc(c_set, 1)
                pool.memset(rep_q[:], 0.0).then_inc(c_set, 1)
                pool.memset(same_head[:], 0.0).then_inc(c_set, 1)
                pool.wait_ge(c_set, 6)
                for m in (ident, identb):
                    pool.affine_select(out=m[:], in_=m[:], compare_op=ALU.not_equal, fill=1.0, base=0,
                                       pattern=[[-1, P]], channel_multiplier=1).then_inc(c_sel, 1)
                for m, n in ((causal, P), (causal8, DSEQ)):
                    pool.affine_select(out=m[:], in_=m[:], compare_op=ALU.is_ge, fill=NEG, base=0,
                                       pattern=[[-1, n]], channel_multiplier=1).then_inc(c_sel, 1)
                pool.affine_select(out=rep_q[:], in_=rep_q[:], compare_op=ALU.not_equal, fill=1.0, base=0,
                                   pattern=[[0, H], [-1, DSEQ]], channel_multiplier=1).then_inc(c_sel, 1)
                pool.affine_select(out=same_head[:], in_=same_head[:], compare_op=ALU.not_equal, fill=1.0,
                                   base=0, pattern=[[-1, H], [0, DSEQ]], channel_multiplier=1).then_inc(c_sel, 1)
                pool.iota(rcnt[:], pattern=[[1, 16]], base=1, channel_multiplier=0,
                          allow_small_or_imprecise_dtypes=True).then_inc(c_iota, 1)
                pool.wait_ge(c_sel, 6)

            @block.vector
            def _(dve):
                dve.memset(eps_col[:], EPS).then_inc(c_dve, 1)
                dve.wait_ge(c_iota, 1)
                dve.reciprocal(rcnt[:], rcnt[:]).then_inc(c_dve, 1)
                dve.wait_ge(c_dve, 2)

        mid = top.enter_context(ExitStack())
        pages = sb(mid, "pages", [1, NSEQ * NPAGES], I32)
        xnT = sb(mid, "xnT", [P, KD, T])
        branch = sb(mid, "branch", [P, 2 * NG * T])
        poolT = branch[:, 0:NG * T].rearrange("p (g t) -> p g t", g=NG)
        attnT = branch[:, NG * T:].rearrange("p (g t) -> p g t", g=NG)
        attn = top.enter_context(ExitStack())
        heads = sb(attn, "heads", [P, 2 * H * SEQ])
        qT, kT = (heads[0:DH + 2, j * H * SEQ:(j + 1) * H * SEQ].rearrange("p (h t) -> p h t", h=H) for j in range(2))
        v_sb = sb(attn, "v_sb", [P, NT + 1, DA])
        qT2 = sb(attn, "qT2", [P, NG, TS])
        kT2 = sb(attn, "kT2", [P, NG, TS])

        with ExitStack() as ctx:
            wqkv = sb(ctx, "wqkv", [P, KD, 3 * DA])
            xb = branch[:, 0:2 * D].rearrange("p (a n) -> p a n", a=2)
            xsc = branch[:, 2 * D:3 * D]
            sqx = branch[:, 3 * D:4 * D]
            xnc = xb.rearrange("p a (c n) -> p a c n", c=KD)
            qk = branch[:, 4 * D:6 * D].rearrange("p (a n) -> p a n", a=2)
            gqk = sb(ctx, "gqk", [P, 2, DH])
            gx = sb(ctx, "gx", [P, KD])
            stx = [sb(ctx, f"stx{i}", [P, 1]) for i in range(4)]
            stq = [sb(ctx, f"stq{i}", [P, 2 * H]) for i in range(4)]
            pT = ps(ctx, "pT", [P, 2, 512])
            pQK = ps(ctx, "pQK", [P, 2, 512])
            pV = ps(ctx, "pV", [P, 512])
            pH = ps(ctx, "pH", [P, 2, 512])

            x_in = [sem("x_in0"), sem("x_in1")]
            w_q_in, w_k_in, w_v_in, gain_in = sem("w_q_in"), sem("w_k_in"), sem("w_v_in"), sem("gain_in")
            sq_done, ms_done, sd_done = sem("sq_done"), sem("ms_done"), sem("sd_done")
            rs_done, xs_done, xT_done = sem("rs_done"), sem("xs_done"), sem("xT_done")
            xnc_done, xnT_done = sem("xnc_done"), sem("xnT_done")
            q_done, k_done, v_done = sem("q_done"), sem("k_done"), sem("v_done")
            sqqk_done, ssq_done, msq_done, sdq_done, rsq_done = (
                sem("sqqk_done"), sem("ssq_done"), sem("msq_done"), sem("sdq_done"), sem("rsq_done"))
            qkn_done, qg_done, qkg_done = sem("qkn_done"), sem("qg_done"), sem("qkg_done")
            hT_done, hT_copied, v_copied = sem("hT_done"), sem("hT_copied"), sem("v_copied")
            kv_out = [sem("kv_out0"), sem("kv_out1")]
            kv_out_s, aug_set = sem("kv_out_s"), sem("aug_set")

            with nc.Block() as block:
                @block.sync
                def _(sp):
                    def load_x(t, i, par, rows):
                        sp.wait_ge(v_done, t + 1)
                        sp.wait_ge(xnT_done, t + 1)
                        src = xp[ds(t * P, rows), :] if rows == P else xs_dram
                        sp.dma_start(xb[0:rows, par, :], src).then_inc(x_in[par], 16)
                    sp.sem_inc(kv_out[0], 32)
                    sp.sem_inc(kv_out[1], 32)
                    sp.dma_start(gqk[:, 0, :], q_norm_g.to_broadcast([P, DH])).then_inc(gain_in, 16)
                    sp.dma_start(gqk[:, 1, :], k_norm_g.to_broadcast([P, DH])).then_inc(gain_in, 16)
                    with nc.allow_non_contiguous_dma(reason="a gain per partition, once"):
                        sp.dma_start(gx[:], norm_mix_g[0].rearrange("(c p) -> p c", p=P)).then_inc(gain_in, 16)
                    sp.dma_start(pages[:], page_table.rearrange("b n -> (b n)").unsqueeze(0)).then_inc(gain_in, 16)
                    with sp.Fori(0, NT // 2) as i:
                        for par in range(2):
                            load_x(i * 2 + par, i, par, P)
                    load_x(NT, NT // 2, 0, TS)

                @block.gpsimd
                def _(pool):
                    pool.sem_inc(xnT_done, 2)
                    for c, s in enumerate((w_q_in, w_k_in, w_v_in)):
                        pool.dma_start(wqkv[:, :, c * DA:(c + 1) * DA],
                                       win[:, :, QKV0 + c * DA:QKV0 + (c + 1) * DA]).then_inc(s, 16)
                    pool.memset(qT[DH:DH + 2, :, :], 1.0).then_inc(aug_set, 1)
                    pool.wait_ge(aug_set, 1)
                    pool.memset(kT[DH:DH + 2, :, :], 1.0).then_inc(aug_set, 1)
                    pool.wait_ge(aug_set, 2)

                    def keep_xn(t, par, rows):
                        pool.wait_ge(xnT_done, t + 2)
                        pool.wait_ge(xnc_done, 2 * t + 4)
                        pool.tensor_copy(xnT[:, :, ds(t * P, rows)], xnc[:, par, :, 0:rows]).then_inc(xnT_done, 1)
                    with pool.Fori(0, NT // 2) as i:
                        for par in range(2):
                            keep_xn(i * 2 + par, par, P)
                    keep_xn(NT, 0, TS)
                    pool.wait_ge(xnT_done, NT + 3)

                @block.scalar
                def _(act):
                    def tile(t, i, par, rows):
                        last = rows != P
                        act.wait_ge(x_in[par], 16 * (i + 1))
                        act.wait_ge(ssq_done, t + 1)
                        act.activation(sqx[0:rows, :], xb[0:rows, par, :], ACT.Square,
                                       accum_out=stx[0][0:rows, :]).then_inc(sq_done, 1)
                        act.wait_ge(ms_done, t + 1)
                        act.activation(stx[2][0:rows, :], stx[1][0:rows, :], ACT.Sqrt).then_inc(sd_done, 1)
                        act.wait_ge(q_done, t + 1)
                        act.wait_ge(k_done, t + 1)
                        act.wait_ge(sq_done, t + 1)
                        act.activation(sqx[0:rows, :], pQK[0:rows, :, :].rearrange("p a b -> p (a b)"),
                                       ACT.Square).then_inc(sqqk_done, 1)
                        act.wait_ge(msq_done, t + 1)
                        act.activation(stq[1][0:rows, :], stq[0][0:rows, :], ACT.Sqrt).then_inc(sdq_done, 1)
                        act.wait_ge(v_done, t + 3)
                        v_tile = v_sb[0:rows, NT, :] if last else v_sb[:, ds(t, 1), :].rearrange("p a b -> p (a b)")
                        act.activation(v_tile, pV[0:rows, :], ACT.Copy).then_inc(v_copied, 1)
                        act.wait_ge(v_copied, t + 2)
                        act.wait_ge(qkg_done, t + 1)
                        if last:
                            act.dma_start(ks_out, qk[0:rows, par, DA:]).then_inc(kv_out_s, 16)
                            act.dma_start(vs_out, v_tile).then_inc(kv_out_s, 16)
                            for j, dst in enumerate((qT2, kT2)):
                                act.wait_ge(hT_done, 2 * NT + j + 5)
                                act.activation(dst[:], pH[:, j, 0:NG * TS].rearrange("p (a b) -> p a b", a=NG),
                                               ACT.Copy).then_inc(hT_copied, 1)
                            act.wait_ge(hT_copied, 4 * NT + 6)
                        else:
                            act.dma_start(kp_out[ds(t * P, P), :], qk[:, par, DA:]).then_inc(kv_out[par], 16)
                            act.dma_start(vp_out[ds(t * P, P), :], v_tile).then_inc(kv_out[par], 16)
                            for j, dst in enumerate((qT, kT)):
                                act.wait_ge(hT_done, 2 * t + j + 5)
                                for e in range(2):
                                    act.activation(dst[0:DH, e:H:2, ds(t * P, P)],
                                                   pH[e * DH:(e + 1) * DH, j, :].rearrange("p (a b) -> p a b", a=4),
                                                   ACT.Copy).then_inc(hT_copied, 1)
                    act.sem_inc(hT_copied, 4)
                    act.sem_inc(v_copied, 1)
                    with act.Fori(0, NT // 2) as i:
                        for par in range(2):
                            tile(i * 2 + par, i, par, P)
                    tile(NT, NT // 2, 0, TS)
                    act.wait_ge(kv_out[0], 32 * (NT // 2 + 1))
                    act.wait_ge(kv_out[1], 32 * (NT // 2 + 1))
                    act.wait_ge(kv_out_s, 32)

                @block.vector
                def _(dve):
                    def tile(t, i, par, rows):
                        dve.wait_ge(sq_done, t + 1)
                        dve.tensor_scalar(stx[1][0:rows, :], stx[0][0:rows, :], 1.0 / D, EPS, ALU.mult,
                                          ALU.add).then_inc(ms_done, 1)
                        dve.wait_ge(sd_done, t + 1)
                        dve.reciprocal(stx[3][0:rows, :], stx[2][0:rows, :]).then_inc(rs_done, 1)
                        dve.wait_ge(rs_done, t + 1)
                        dve.wait_ge(xT_done, 2 * t + 2)
                        dve.tensor_scalar(xsc[0:rows, :], xb[0:rows, par, :], stx[3][0:rows, :], None,
                                          ALU.mult).then_inc(xs_done, 1)
                        dve.wait_ge(xs_done, t + 1)
                        for j in range(2):
                            dve.wait_ge(xT_done, 2 * t + j + 3)
                            dve.tensor_tensor(xnc[:, par, 4 * j:4 * j + 4, 0:rows],
                                              pT[:, j, :].rearrange("p (a b) -> p a b", a=4)[:, :, 0:rows],
                                              gx[:, 4 * j:4 * j + 4].unsqueeze(2).to_broadcast([P, 4, rows]),
                                              ALU.mult).then_inc(xnc_done, 1)
                        dve.wait_ge(sqqk_done, t + 1)
                        dve.tensor_reduce(stq[2][0:rows, :], sqx[0:rows, :].rearrange("p (h d) -> p h d", d=DH),
                                          AX.X, ALU.add).then_inc(ssq_done, 1)
                        dve.wait_ge(ssq_done, t + 2)
                        dve.tensor_scalar(stq[0][0:rows, :], stq[2][0:rows, :], 1.0 / DH, EPS, ALU.mult,
                                          ALU.add).then_inc(msq_done, 1)
                        dve.wait_ge(sdq_done, t + 1)
                        dve.reciprocal(stq[3][0:rows, :], stq[1][0:rows, :]).then_inc(rsq_done, 1)
                        dve.wait_ge(rsq_done, t + 1)
                        dve.wait_ge(kv_out[par], 32 * i + 32)
                        dve.wait_ge(hT_done, 2 * t + 2)
                        dve.tensor_tensor(qk[0:rows, par, :].rearrange("p (h d) -> p h d", d=DH),
                                          pQK[0:rows, :, :].rearrange("p a (h d) -> p (a h) d", d=DH),
                                          stq[3][0:rows, :].unsqueeze(2).to_broadcast([rows, 2 * H, DH]),
                                          ALU.mult).then_inc(qkn_done, 1)
                        dve.wait_ge(qkn_done, t + 2)
                        for j, s in enumerate((qg_done, qkg_done)):
                            half = qk[0:rows, par, j * DA:(j + 1) * DA].rearrange("p (h d) -> p h d", d=DH)
                            dve.tensor_tensor(half, half, gqk[0:rows, j, :].unsqueeze(1).to_broadcast([rows, H, DH]),
                                              ALU.mult).then_inc(s, 1)
                    dve.sem_inc(xnc_done, 2)
                    dve.sem_inc(qkn_done, 1)
                    dve.sem_inc(ssq_done, 1)
                    dve.wait_ge(gain_in, 64)
                    with dve.Fori(0, NT // 2) as i:
                        for par in range(2):
                            tile(i * 2 + par, i, par, P)
                    tile(NT, NT // 2, 0, TS)

                @block.tensor
                def _(pe):
                    def tile(t, i, par, rows):
                        pe.wait_ge(xs_done, t + 1)
                        for j in range(2):
                            pe.wait_ge(xnc_done, 2 * t + j + 1)
                            for a in range(4):
                                c = 4 * j + a
                                ins = pe.transpose(pT[:, j, a * P:a * P + rows], xsc[0:rows, c * P:(c + 1) * P],
                                                   ident[0:rows, 0:rows])
                            ins.then_inc(xT_done, 1)
                        pe.wait_ge(xnc_done, 2 * t + 4)
                        for n, (out, w_in_sem, done) in enumerate(((pQK[0:rows, 0, :], w_q_in, q_done),
                                                                   (pQK[0:rows, 1, :], w_k_in, k_done),
                                                                   (pV[0:rows, :], w_v_in, v_done))):
                            pe.wait_ge(w_in_sem, 16)
                            if n == 0:
                                pe.wait_ge(qkn_done, t + 1)
                            if n == 2:
                                pe.wait_ge(v_copied, t + 1)
                            for c in range(KD):
                                ins = pe.matmul(out, xnc[:, par, c, 0:rows], wqkv[:, c, n * DA:(n + 1) * DA],
                                                start=(c == 0), stop=(c == KD - 1))
                            ins.then_inc(done, 1)
                        pe.wait_ge(qg_done, t + 1)
                        pe.wait_ge(qkg_done, t + 1)
                        for j in range(2):
                            pe.wait_ge(hT_copied, 4 * t + 2 * j + 2)
                            for a in range(NG):
                                col = (NG * j + a) * P
                                ins = pe.transpose(pH[:, j, a * rows:(a + 1) * rows],
                                                   qk[0:rows, par, col:col + P], ident[0:rows, 0:rows])
                            ins.then_inc(hT_done, 1)
                    pe.sem_inc(v_done, 2)
                    pe.sem_inc(xT_done, 2)
                    pe.sem_inc(hT_done, 4)
                    with pe.Fori(0, NT // 2) as i:
                        for par in range(2):
                            tile(i * 2 + par, i, par, P)
                    tile(NT, NT // 2, 0, TS)

        n_project = len(in_use)
        late = attn.enter_context(ExitStack())
        logfT = sb(late, "logfT", [H, T])
        with ExitStack() as ctx:
            PAD = POOL_WINDOWS[-1]
            EXT = HIST + DSEQ
            wf = sb(ctx, "wf", [P, KD, H])
            wu = sb(ctx, "wu", [P, KD, P * NG])
            mixw = sb(ctx, "mixw", [P, NG, P])
            pscale = sb(ctx, "pscale", [P, NG])
            bf = sb(ctx, "bf", [H, 1])
            fz = sb(ctx, "fz", [H, T])
            fe = sb(ctx, "fe", [H, T])
            cT = sb(ctx, "cT", [H, SEQ])
            rows_tmp = sb(ctx, "rows_tmp", [P, 2 * DP])
            ones_row = rows_tmp[0:H, 0:SEQ]
            ph, pn = rows_tmp[0:HIST, 0:DP], rows_tmp[0:TS, DP:]
            lf_rows = sb(ctx, "lf_rows", [P, NT + 1, H])
            hist = sb(ctx, "hist", [NSEQ * HIST, DP])
            ue = sb(ctx, "ue", [P, 2, PAD + SEQ])
            us = sb(ctx, "us", [P, 2, NSEQ, EXT])
            un = sb(ctx, "un", [P, 2, TS])
            wa = attnT.rearrange("p g t -> p (g t)")[:, 0:2 * (PAD + SEQ)].rearrange(
                "p (a n) -> p a n", a=2)
            wsm = sb(ctx, "wsm", [P, 2, NSEQ, EXT])
            fix = sb(ctx, "fix", [P, PAD])
            mt = attnT.rearrange("p g t -> p (g t)")[:, 2 * (PAD + SEQ):2 * (PAD + SEQ + T)].rearrange(
                "p (a n) -> p a n", a=2)
            pF = ps(ctx, "pF", [P, 3, 512])
            pM = ps(ctx, "pM", [P, 3, 512])
            pX = ps(ctx, "pX", [P, 512])
            pO2 = ps(ctx, "pO2", [P, 512])

            w_in_done, f_in, hist_in = sem("wu_in"), sem("f_in"), sem("hist_in")
            f_mm, f_z, f_abs, f_exp, f_ln, f_min, f_sub = (
                sem("f_mm"), sem("f_z"), sem("f_abs"), sem("f_exp"), sem("f_ln"), sem("f_min"), sem("f_sub"))
            ones_set, scanned, c_scaled, aug_in = sem("ones_set"), sem("scanned"), sem("c_scaled"), sem("aug_in")
            lfT_done, lf_copied, lf_out = sem("lfT_done"), sem("lf_copied"), sem("lf_out")
            pad_set, u_done, u_copied = sem("pad_set"), sem("u_done"), sem("u_copied")
            hx_done, hx_copied = sem("hx_done"), sem("hx_copied")
            pool_step, m_done, mix_done, mix_copied = sem("pool_step"), sem("m_done"), sem("mix_done"), sem("mix_copied")
            pt_done, pt_copied, pool_out = sem("pt_done"), sem("pt_copied"), sem("pool_out")

            finished = [s for s in in_use[:n_project] if all(s is not w for w in (w_q_in, w_k_in, w_v_in))]
            with nc.Block() as block:
                @block.gpsimd
                def _(pool):
                    for s in finished:
                        pool.sem_clear(s)

                @block.sync
                def _(sp):
                    with nc.allow_non_contiguous_dma(reason="eight forget columns, a scale per partition, once"):
                        sp.dma_start(wf[:], win[:, :, F0:F0 + H]).then_inc(f_in, 16)
                        sp.dma_start(bf[:], b_forget.rearrange("a h -> h a")).then_inc(f_in, 16)
                        sp.dma_start(pscale[:], pool_scale[0].rearrange("(g p) -> p g", p=P)).then_inc(f_in, 16)
                    sp.dma_start(wu[:], win[:, :, 0:DP]).then_inc(w_in_done, 16)
                    sp.dma_start(mixw[:], pool_mix_w[0].rearrange("g c d -> c g d")).then_inc(f_in, 16)
                    sp.dma_start(hist[:], state_pool[0].rearrange("b t c -> (b t) c")).then_inc(hist_in, 16)
                    sp.dma_start(pool_sample[0][:, 0:HIST - DSEQ, :], state_pool[0][:, DSEQ:HIST, :]).then_inc(pool_out, 16)
                    sp.wait_ge(c_scaled, 2)
                    sp.dma_start(qT[DH:DH + 1, :, :], fz[:, 0:SEQ]).then_inc(aug_in, 16)
                    sp.dma_start(kT[DH + 1:DH + 2, :, :], fe[:, 0:SEQ]).then_inc(aug_in, 16)
                    sp.wait_ge(lf_copied, 1)
                    sp.dma_start(lfp_out, lf_rows[:, 0:NT, :]).then_inc(lf_out, 16)
                    sp.dma_start(lfs_out, lf_rows[0:TS, NT, :]).then_inc(lf_out, 16)
                    sp.wait_ge(pt_copied, 2 * NG)
                    sp.dma_start(pool_prompt[0, 0], ph).then_inc(pool_out, 16)
                    for b in range(NSEQ):
                        sp.dma_start(pool_sample[0][b, HIST - DSEQ:HIST, :],
                                     pn[b * DSEQ:(b + 1) * DSEQ, :]).then_inc(pool_out, 16)
                    sp.wait_ge(aug_in, 32)
                    sp.wait_ge(lf_out, 32)
                    sp.wait_ge(pool_out, 16 * (2 + NSEQ))

                def mix(pe, g):
                    pe.wait_ge(lf_copied, 1)
                    pe.wait_ge(u_copied, 4 * g + 4)
                    if g:
                        pe.wait_ge(pt_copied, 2 * g)
                    pe.transpose(pO2[0:HIST, 0:P], ue[:, g % 2, PAD + SEQ - HIST:], ident[:])
                    pe.transpose(pO2[0:TS, P:2 * P], un[:, g % 2, :], ident[:]).then_inc(pt_done, 1)
                    pe.wait_ge(m_done, g + 1)
                    if g:
                        pe.wait_ge(mix_copied, 3 * g)
                    for n, (c0, cn) in enumerate(COLS):
                        pe.matmul(pM[:, n, 0:cn], mixw[:, g, :], mt[:, g % 2, c0:c0 + cn],
                                  start=True, stop=True).then_inc(mix_done, 1)

                @block.tensor
                def _(pe):
                    pe.wait_ge(f_in, 64)
                    for n, (c0, cn) in enumerate(COLS):
                        for c in range(KD):
                            ins = pe.matmul(pF[0:H, n, 0:cn], wf[:, c, :], xnT[:, c, c0:c0 + cn],
                                            start=(c == 0), stop=(c == KD - 1))
                    ins.then_inc(f_mm, 1)
                    pe.wait_ge(hist_in, 16)
                    pe.wait_ge(w_in_done, 16)
                    for g in range(NG):
                        if g:
                            pe.wait_ge(hx_copied, g)
                        pe.transpose(pX[:, 0:NSEQ * HIST], hist[:, g * P:(g + 1) * P],
                                     ident[0:NSEQ * HIST, 0:NSEQ * HIST]).then_inc(hx_done, 1)
                        pe.wait_ge(f_z, 1)
                        pe.wait_ge(u_copied, 4 * g) if g else None
                        for n, (c0, cn) in enumerate(COLS):
                            for c in range(KD):
                                ins = pe.matmul(pF[:, n, 0:cn], wu[:, c, g * P:(g + 1) * P],
                                                xnT[:, c, c0:c0 + cn], start=(c == 0), stop=(c == KD - 1))
                        ins.then_inc(u_done, 1)
                        if g:
                            mix(pe, g - 1)
                        else:
                            pe.wait_ge(f_sub, 1)
                            for n in range(NT + 1):
                                rows = P if n < NT else TS
                                ins = pe.transpose(pO2[0:rows, n * H:(n + 1) * H], logfT[:, n * P:n * P + rows],
                                                   ident[0:H, 0:H])
                            ins.then_inc(lfT_done, 1)
                    mix(pe, NG - 1)

                def mixed(act, g):
                    for n, (c0, cn) in enumerate(COLS):
                        act.wait_ge(mix_done, 3 * g + n + 1)
                        act.activation(poolT[:, g, c0:c0 + cn], pM[:, n, 0:cn], ACT.Copy,
                                       scale=pscale[:, g:g + 1]).then_inc(mix_copied, 1)

                @block.scalar
                def _(act):
                    act.wait_ge(f_in, 64)
                    act.wait_ge(f_mm, 1)
                    for n, (c0, cn) in enumerate(COLS):
                        ins = act.activation(fz[:, c0:c0 + cn], pF[0:H, n, 0:cn], ACT.Identity, bias=bf[:])
                    ins.then_inc(f_z, 1)
                    act.wait_ge(f_z, 1)
                    act.activation(fe[:], fz[:], ACT.Abs).then_inc(f_abs, 1)
                    act.wait_ge(f_abs, 1)
                    act.activation(fe[:], fe[:], ACT.Exp, scale=-1.0).then_inc(f_exp, 1)
                    act.wait_ge(f_exp, 1)
                    act.activation(fe[:], fe[:], ACT.Ln, bias=1.0).then_inc(f_ln, 1)
                    act.wait_ge(pad_set, 1)
                    for g in range(NG):
                        act.wait_ge(hx_done, g + 1)
                        if g >= 2:
                            act.wait_ge(m_done, g - 1)
                            act.wait_ge(pt_done, g - 1)
                        act.activation(us[:, g % 2, :, 0:HIST],
                                       pX[:, 0:NSEQ * HIST].rearrange("p (b t) -> p b t", t=HIST),
                                       ACT.Copy).then_inc(hx_copied, 1)
                        act.wait_ge(u_done, g + 1)
                        act.activation(ue[:, g % 2, PAD:PAD + SEQ], pF[:, 0:2, :].rearrange("p a b -> p (a b)"),
                                       ACT.Copy).then_inc(u_copied, 2)
                        act.activation(us[:, g % 2, :, HIST:EXT],
                                       pF[:, 2, 0:TS].rearrange("p (b t) -> p b t", t=DSEQ),
                                       ACT.Copy).then_inc(u_copied, 1)
                        act.activation(un[:, g % 2, :], pF[:, 2, 0:TS], ACT.Copy).then_inc(u_copied, 1)
                        if g:
                            mixed(act, g - 1)
                    mixed(act, NG - 1)

                @block.vector
                def _(dve):
                    n_step = [0]

                    def step(ins):
                        n_step[0] += 1
                        ins.then_inc(pool_step, 1)
                        dve.wait_ge(pool_step, n_step[0])

                    dve.memset(ones_row, 1.0).then_inc(ones_set, 1)
                    dve.memset(ue[:, :, 0:PAD], 0.0).then_inc(pad_set, 1)
                    dve.wait_ge(f_z, 1)
                    dve.tensor_scalar(logfT[:], fz[:], 0.0, None, ALU.min).then_inc(f_min, 1)
                    dve.wait_ge(f_min, 1)
                    dve.wait_ge(f_ln, 1)
                    dve.tensor_tensor(logfT[:], logfT[:], fe[:], ALU.subtract).then_inc(f_sub, 1)
                    dve.wait_ge(f_sub, 1)
                    dve.wait_ge(ones_set, 1)
                    dve.tensor_tensor_scan(cT[:], ones_row, logfT[:, 0:SEQ], 0.0, ALU.mult,
                                           ALU.add).then_inc(scanned, 1)
                    dve.wait_ge(scanned, 1)
                    dve.tensor_scalar(fz[:, 0:SEQ], cT[:], INV, None, ALU.mult).then_inc(c_scaled, 1)
                    dve.tensor_scalar(fe[:, 0:SEQ], cT[:], -INV, None, ALU.mult).then_inc(c_scaled, 1)
                    dve.wait_ge(lfT_done, 1)
                    dve.tensor_copy(lf_rows[:, 0:NT, :], pO2[:, 0:NT * H].rearrange("p (n h) -> p n h", h=H))
                    dve.tensor_copy(lf_rows[0:TS, NT, :], pO2[0:TS, NT * H:(NT + 1) * H]).then_inc(lf_copied, 1)
                    for g in range(NG):
                        w = POOL_WINDOWS[g]
                        dve.wait_ge(u_copied, 4 * g + 4)
                        dve.wait_ge(hx_copied, g + 1)
                        src, srcs, first = ue[:, g % 2, :], us[:, g % 2], 0
                        for lvl in range(g + 1):
                            h = 1 << lvl
                            first += h
                            dst, dsts = wa[:, lvl % 2, :], wsm[:, lvl % 2]
                            dve.tensor_tensor(dst[:, first:], src[:, first:], src[:, first - h:PAD + SEQ - h],
                                              ALU.add)
                            step(dve.tensor_tensor(dsts[:, :, first:], srcs[:, :, first:],
                                                   srcs[:, :, first - h:EXT - h], ALU.add))
                            src, srcs = dst, dsts
                        if g >= 2:
                            dve.wait_ge(mix_done, 3 * (g - 1))
                        m = mt[:, g % 2, :]
                        dve.scalar_tensor_tensor(m[:, SEQ:].rearrange("p (b t) -> p b t", t=DSEQ),
                                                 srcs[:, :, HIST:], 1.0 / w, us[:, g % 2, :, HIST:],
                                                 ALU.mult, ALU.subtract)
                        step(dve.scalar_tensor_tensor(m[:, 0:SEQ], src[:, PAD:], 1.0 / w, ue[:, g % 2, PAD:],
                                                      ALU.mult, ALU.subtract))
                        step(dve.tensor_tensor(fix[:, 0:w - 1], src[:, PAD:PAD + w - 1], rcnt[:, 0:w - 1], ALU.mult))
                        dve.tensor_tensor(m[:, 0:w - 1], fix[:, 0:w - 1], ue[:, g % 2, PAD:PAD + w - 1],
                                          ALU.subtract).then_inc(m_done, 1)
                        dve.wait_ge(m_done, g + 1)
                        dve.wait_ge(pt_done, g + 1)
                        dve.tensor_copy(ph[:, g * P:(g + 1) * P], pO2[0:HIST, 0:P]).then_inc(pt_copied, 1)
                        dve.tensor_copy(pn[:, g * P:(g + 1) * P], pO2[0:TS, P:2 * P]).then_inc(pt_copied, 1)

        NB = NT
        UNITS = [NB - 1 - u for u in range(NB)]
        GROUPS = []
        for u, qb in enumerate(UNITS):
            GROUPS += [(u, k0, min(4, qb + 1 - k0)) for k0 in range(0, qb + 1, 4)]
        NGR = len(GROUPS)
        GEND = [max(i for i, x in enumerate(GROUPS) if x[0] == u) + 1 for u in range(NB)]
        assert NGR % 2 == 0
        spare += finished
        with ExitStack() as ctx:
            qh = sb(ctx, "qh", [DH + 2, SEQ])
            prob = sb(ctx, "prob", [P, 2, SEQ])
            probT = sb(ctx, "probT", [P, 2, SEQ])
            o_rows = sb(ctx, "o_rows", [P, NB, DA])
            mx = sb(ctx, "mx", [P, 2])
            nmx = sb(ctx, "nmx", [P, 2])
            rsum = sb(ctx, "rsum", [P, 4])
            rinv = sb(ctx, "rinv", [P, 1])
            pS = ps(ctx, "pS", [P, 2, 2, 512])
            pPT = ps(ctx, "pPT", [P, 2, 512])
            pO = ps(ctx, "pO", [P, 2, 512])

            qh_ready, s_done, mx_done, nmx_done = sem("qh_ready"), sem("s_done"), sem("mx_done"), sem("nmx_done")
            p_done, t_done, pv_done = sem("p_done"), sem("t_done"), sem("pv_done")
            turned = [sem("turned0"), sem("turned1")]
            rinv_done, o_done = sem("rinv_done"), sem("o_done")
            oT_done, oT_copied = sem("oT_done"), sem("oT_copied")

            def copy_groups(eng, h, u, par):
                for r, (ru, k0, kn) in enumerate(GROUPS):
                    if ru != u or r % 2 != par:
                        continue
                    eng.wait_ge(t_done, NGR * h + r + NGR + 1)
                    eng.wait_ge(pv_done, NB * h + u + 1)
                    dst, src = probT[:, u % 2, k0 * P:(k0 + kn) * P], pPT[:, par, 0:kn * P]
                    if par:
                        eng.activation(dst, src, ACT.Copy).then_inc(turned[1], 1)
                    else:
                        eng.tensor_copy(dst, src).then_inc(turned[0], 1)

            with nc.Block() as block:
                @block.gpsimd
                def _(pool):
                    with pool.Fori(0, H) as h:
                        pool.wait_ge(s_done, NB * h + 8)
                        pool.tensor_copy(qh[:], qT[:, ds(h, 1), :].rearrange("p a t -> p (a t)")).then_inc(qh_ready, 1)
                        pool.wait_ge(qh_ready, h + 1)

                @block.tensor
                def _(pe):
                    def scores(h, u):
                        n = (UNITS[u] + 1) * P
                        pe.wait_ge(qh_ready, h + 1)
                        pe.wait_ge(p_done, NB * h + u + 1)
                        lhsT = qh[:, n - P:n]
                        out = pS[:, u % 2].rearrange("p a b -> p (a b)")
                        for c0 in range(0, n - P, 512):
                            c1 = min(c0 + 512, n - P)
                            pe.matmul(out[:, c0:c1], lhsT, kT[:, ds(h, 1), c0:c1].rearrange("p a t -> p (a t)"),
                                      start=True, stop=True)
                        pe.matmul(out[:, n - P:n], lhsT, kT[:, ds(h, 1), n - P:n].rearrange("p a t -> p (a t)"),
                                  start=True, stop=False)
                        pe.matmul(out[:, n - P:n], identb[:], causal[:], start=False, stop=True).then_inc(s_done, 1)

                    def turn(h, u):
                        pe.wait_ge(p_done, NB * h + u + 3)
                        for r, (ru, k0, kn) in enumerate(GROUPS):
                            if ru != u:
                                continue
                            pe.wait_ge(turned[r % 2], NGR // 2 * h + r // 2 + 1)
                            for a in range(kn):
                                ins = pe.transpose(pPT[:, r % 2, a * P:(a + 1) * P],
                                                   prob[:, u % 2, (k0 + a) * P:(k0 + a + 1) * P], ident[:])
                            ins.then_inc(t_done, 1)

                    def weigh(h, u):
                        pe.wait_ge(o_done, NB * h + u + 3)
                        for r, (ru, k0, kn) in enumerate(GROUPS):
                            if ru != u:
                                continue
                            pe.wait_ge(turned[r % 2], NGR // 2 * h + r // 2 + 2)
                            for kb in range(k0, k0 + kn):
                                ins = pe.matmul(pO[:, u % 2, 0:DH], probT[:, u % 2, kb * P:(kb + 1) * P],
                                                v_sb[:, kb, ds(h * DH, DH)], start=(kb == 0), stop=(kb == UNITS[u]))
                        ins.then_inc(pv_done, 1)
                    pe.sem_inc(s_done, 8)
                    pe.sem_inc(t_done, NGR)
                    pe.sem_inc(pv_done, 2)
                    with pe.Fori(0, H) as h:
                        scores(h, 0)
                        for u in range(NB):
                            if u + 1 < NB:
                                scores(h, u + 1)
                            if u:
                                weigh(h, u - 1)
                            turn(h, u)
                        weigh(h, NB - 1)
                    pe.wait_ge(o_done, NB * H + 4)
                    for qb in range(NB):
                        if qb >= 2:
                            pe.wait_ge(oT_copied, qb - 1)
                        for g in range(NG):
                            ins = pe.transpose(pPT[:, qb % 2, g * P:(g + 1) * P], o_rows[:, qb, g * P:(g + 1) * P],
                                               ident[:])
                        ins.then_inc(oT_done, 1)

                @block.scalar
                def _(act):
                    def exps(h, u):
                        n = (UNITS[u] + 1) * P
                        act.wait_ge(nmx_done, NB * h + u + 1)
                        act.wait_ge(t_done, NGR * h + (GEND[u - 2] + NGR if u >= 2 else GEND[u + NB - 2]))
                        act.wait_ge(o_done, NB * h + u + 1)
                        act.activation(prob[:, u % 2, 0:n], pS[:, u % 2].rearrange("p a b -> p (a b)")[:, 0:n],
                                       ACT.Exp, bias=nmx[:, u % 2:u % 2 + 1], scale=SCALE,
                                       accum_out=rsum[:, u % 4:u % 4 + 1]).then_inc(p_done, 1)
                    act.sem_inc(p_done, 2)
                    act.sem_inc(turned[1], 1)
                    with act.Fori(0, H) as h:
                        exps(h, 0)
                        for u in range(NB):
                            if u + 1 < NB:
                                exps(h, u + 1)
                            copy_groups(act, h, u, 1)
                    for qb in range(1, NB, 2):
                        act.wait_ge(oT_done, qb + 1)
                        act.wait_ge(oT_copied, qb)
                        act.activation(attnT[:, :, qb * P:(qb + 1) * P],
                                       pPT[:, 1, :].rearrange("p (g q) -> p g q", g=NG), ACT.Copy).then_inc(oT_copied, 1)

                @block.vector
                def _(dve):
                    def maxes(h, u):
                        n = (UNITS[u] + 1) * P
                        dve.wait_ge(s_done, NB * h + u + 9)
                        dve.tensor_reduce(mx[:, u % 2:u % 2 + 1], pS[:, u % 2].rearrange("p a b -> p (a b)")[:, 0:n],
                                          AX.X, ALU.max).then_inc(mx_done, 1)
                        dve.wait_ge(mx_done, NB * h + u + 1)
                        dve.tensor_scalar(nmx[:, u % 2:u % 2 + 1], mx[:, u % 2:u % 2 + 1], -SCALE, None,
                                          ALU.mult).then_inc(nmx_done, 1)

                    def outputs(h, u):
                        dve.wait_ge(pv_done, NB * h + u + 3)
                        dve.wait_ge(o_done, NB * h + u + 4)
                        dve.reciprocal(rinv[:], rsum[:, u % 4:u % 4 + 1]).then_inc(rinv_done, 1)
                        dve.wait_ge(rinv_done, NB * h + u + 1)
                        dve.tensor_scalar(o_rows[:, UNITS[u], ds(h * DH, DH)], pO[:, u % 2, 0:DH], rinv[:], None,
                                          ALU.mult).then_inc(o_done, 1)
                    dve.sem_inc(o_done, 4)
                    dve.sem_inc(turned[0], 1)
                    with dve.Fori(0, H) as h:
                        maxes(h, 0)
                        for u in range(NB):
                            if u + 1 < NB:
                                maxes(h, u + 1)
                            if u:
                                outputs(h, u - 1)
                            copy_groups(dve, h, u, 0)
                        outputs(h, NB - 1)
                    for qb in range(0, NB, 2):
                        dve.wait_ge(oT_done, qb + 1)
                        if qb:
                            dve.wait_ge(oT_copied, qb)
                        dve.tensor_copy(attnT[:, :, qb * P:(qb + 1) * P],
                                        pPT[:, 0, :].rearrange("p (g q) -> p g q", g=NG)).then_inc(oT_copied, 1)

        with ExitStack() as ctx:
            kp, vp = (heads[:, j * 2 * PAST * NG:(j + 1) * 2 * PAST * NG].rearrange(
                "p (a n c) -> p a n c", a=2, n=NPAGES) for j in range(2))
            kpT = heads[:, 4 * PAST * NG:5 * PAST * NG].rearrange("p (g k) -> p g k", g=NG)
            lfp = sb(ctx, "lfp", [P, 2, NPAGES, H])
            vn = sb(ctx, "vn", [DSEQ, 2, DA])
            lfr = sb(ctx, "lfr", [H, ALLK])
            cr = sb(ctx, "cr", [H, ALLK])
            ncr = sb(ctx, "ncr", [H, ALLK])
            ones = sb(ctx, "ones", [H, ALLK])
            cq = sb(ctx, "cq", [H, DSEQ])
            cq_rows = sb(ctx, "cq_rows", [H, H, DSEQ])
            qbd = sb(ctx, "qbd", [P, NG * (H * DSEQ + 2 * DSEQ)])
            pr = sb(ctx, "pr", [TS, ALLK])
            prn = sb(ctx, "prn", [P, ALLK])
            prT = sb(ctx, "prT", [P, (NPAGES + 1) * TS])
            dmx = [sb(ctx, f"dmx{i}", [TS, 1]) for i in range(4)]
            pC = ps(ctx, "pC", [P, 512])
            pK = ps(ctx, "pK", [P, 2, 512])
            pSS = ps(ctx, "pSS", [P, 1024])
            pP = ps(ctx, "pP", [P, 512])
            pOO = ps(ctx, "pOO", [P, 512])

            k_in = [sem("k_in0"), sem("k_in1")]
            vc_in = [sem("vc_in0"), sem("vc_in1")]
            lf_in = [sem("lf_in0"), sem("lf_in1")]
            d_set, lT_done, lT_copied, lr_new = sem("d_set"), sem("lT_done"), sem("lT_copied"), sem("lr_new")
            d_scan, d_ncr, d_cq, d_rows, qbd_done = sem("d_scan"), sem("d_ncr"), sem("d_cq"), sem("d_rows"), sem("qbd_done")
            kT_done, kT_copied = sem("kT_done"), [sem("kT_copied0"), sem("kT_copied1")]
            ds_done, dmx_done, dnm_done, de_done = sem("ds_done"), sem("dmx_done"), sem("dnm_done"), sem("de_done")
            dr_done, dn_done, dT_done, dT_copied = sem("dr_done"), sem("dn_done"), sem("dT_done"), sem("dT_copied")
            do_done, do_copied = sem("do_done"), sem("do_copied")

            with nc.Block() as block:
                @block.sync
                def _(sp):
                    with sp.Fori(0, NSEQ // 2) as i:
                        for par in range(2):
                            b = 2 * i + par
                            pg = [sp.value_load(pages[0:1, ds(b * NPAGES + j, 1)], min_val=0, max_val=NPHYS - 1)
                                  for j in range(NPAGES)]
                            sp.wait_ge(lT_done, b + 1)
                            for j in range(NPAGES):
                                sp.dma_start(lfp[:, par, j, :], clf[ds(pg[j], 1)].rearrange("a t h -> (a t) h")
                                             ).then_inc(lf_in[par], 16)
                            sp.wait_ge(kT_done, 4 * b + 4)
                            for j in range(NPAGES):
                                sp.dma_start(kp[:, par, j, :], ck[ds(pg[j], 1)].rearrange("a t n -> (a t) n")
                                             ).then_inc(k_in[par], 16)
                            sp.wait_ge(do_done, b + 1)
                            for j in range(NPAGES):
                                sp.dma_start(vp[:, par, j, :], cv[ds(pg[j], 1)].rearrange("a t n -> (a t) n")
                                             ).then_inc(vc_in[par], 16)
                            sp.dma_start(vn[:, par, :], vs_out[ds(b * DSEQ, DSEQ), :]).then_inc(vc_in[par], 16)

                @block.tensor
                def _(pe):
                    def sequence(b, i, par):
                        pe.wait_ge(lf_in[par], 16 * NPAGES * (i + 1))
                        pe.wait_ge(lT_copied, b + 1)
                        for j in range(NPAGES):
                            ins = pe.transpose(pC[0:H, j * P:(j + 1) * P], lfp[:, par, j, :], ident[:])
                        ins.then_inc(lT_done, 1)
                        pe.wait_ge(k_in[par], 16 * NPAGES * (i + 1))
                        for p in range(NG):
                            pe.wait_ge(kT_copied[p % 2], 2 * b + p // 2 + 1)
                            for j in range(NPAGES):
                                ins = pe.transpose(pK[:, p % 2, j * P:(j + 1) * P],
                                                   kp[:, par, j, p * P:(p + 1) * P], ident[:])
                            ins.then_inc(kT_done, 1)
                        pe.wait_ge(qbd_done, b + 1)
                        pe.wait_ge(d_rows, b + 1)
                        pe.wait_ge(de_done, b + 1)
                        for part in range(2):
                            out = pSS[0:TS, 0:PAST] if part == 0 else pSS[0:TS, PAST:ALLK]
                            for p in range(NG):
                                if part == 0:
                                    pe.wait_ge(kT_copied[p % 2], 2 * b + p // 2 + 2)
                                rhs = kpT[:, p, :] if part == 0 else kT2[:, p, ds(b * DSEQ, DSEQ)]
                                pe.matmul(out, qbd[:, p * TS:(p + 1) * TS], rhs, start=(p == 0), stop=False)
                            cols = slice(0, PAST) if part == 0 else slice(PAST, ALLK)
                            pe.matmul(out, same_head[:].rearrange("p h q -> p (h q)"), ncr[:, cols],
                                      start=False, stop=False)
                            ins = pe.matmul(out, cq_rows[:].rearrange("p h q -> p (h q)"), ones[:, cols],
                                            start=False, stop=(part == 0))
                        pe.matmul(out, rep_q[:].rearrange("p h q -> p (h q)"), causal8[:], start=False,
                                  stop=True).then_inc(ds_done, 1)
                        pe.wait_ge(dn_done, b + 1)
                        pe.wait_ge(dT_copied, b + 1)
                        for j in range(NPAGES):
                            pe.matmul(pP[:, j * TS:(j + 1) * TS], prn[:, j * P:(j + 1) * P], ident[:, 0:TS],
                                      start=True, stop=True)
                        pe.matmul(pP[0:DSEQ, NPAGES * TS:(NPAGES + 1) * TS], prn[:, PAST:ALLK],
                                  ident[:, 0:TS], start=True, stop=True).then_inc(dT_done, 1)
                        pe.wait_ge(vc_in[par], 16 * (NPAGES + 1) * (i + 1))
                        pe.wait_ge(dT_copied, b + 2)
                        pe.wait_ge(do_copied, b + 1)
                        for h in range(H):
                            out = pOO[0:DH, h * DSEQ:(h + 1) * DSEQ]
                            for j in range(NPAGES):
                                pe.matmul(out, vp[:, par, j, h * DH:(h + 1) * DH],
                                          prT[:, j * TS + h * DSEQ:j * TS + (h + 1) * DSEQ], start=(j == 0), stop=False)
                            ins = pe.matmul(out, vn[:, par, h * DH:(h + 1) * DH],
                                            prT[0:DSEQ, NPAGES * TS + h * DSEQ:NPAGES * TS + (h + 1) * DSEQ],
                                            start=False, stop=True)
                        ins.then_inc(do_done, 1)
                    pe.sem_inc(kT_done, 8)
                    pe.sem_inc(do_done, 2)
                    pe.sem_inc(lT_done, 2)
                    pe.wait_ge(d_set, 3)
                    pe.sem_inc(ds_done, 1)
                    pe.sem_inc(dT_done, 1)
                    with pe.Fori(0, NSEQ // 2) as i:
                        for par in range(2):
                            sequence(2 * i + par, i, par)

                @block.scalar
                def _(act):
                    act.sem_inc(kT_copied[1], 1)
                    act.sem_inc(de_done, 1)
                    with act.Fori(0, NSEQ) as b:
                        for p in (1, 3):
                            act.wait_ge(kT_done, 4 * b + p + 9)
                            act.wait_ge(ds_done, b + 1)
                            act.activation(kpT[:, p, :], pK[:, 1, :], ACT.Copy).then_inc(kT_copied[1], 1)
                        act.wait_ge(dnm_done, b + 1)
                        act.activation(pr[:], pSS[0:TS, 0:ALLK], ACT.Exp, bias=dmx[1][:], scale=SCALE,
                                       accum_out=dmx[2][:]).then_inc(de_done, 1)

                @block.vector
                def _(dve):
                    dve.memset(ones[:], 1.0).then_inc(d_set, 1)
                    dve.memset(qbd[:], 0.0).then_inc(d_set, 1)
                    dve.memset(prn[:], 0.0).then_inc(d_set, 1)
                    dve.wait_ge(d_set, 3)
                    dve.sem_inc(lT_copied, 1)
                    dve.sem_inc(kT_copied[0], 1)
                    dve.sem_inc(dT_copied, 1)
                    dve.sem_inc(do_copied, 1)
                    qcols = qbd[:].rearrange("p (g s) -> p g s", s=TS + 2 * DSEQ)
                    with dve.Fori(0, NSEQ) as b:
                        dve.wait_ge(lT_done, b + 3)
                        dve.tensor_copy(lfr[:, 0:PAST], pC[0:H, :]).then_inc(lT_copied, 1)
                        dve.tensor_copy(lfr[:, PAST:ALLK], logfT[:, ds(SEQ + b * DSEQ, DSEQ)]).then_inc(lr_new, 1)
                        dve.wait_ge(lT_copied, b + 2)
                        dve.wait_ge(lr_new, b + 1)
                        dve.tensor_tensor_scan(cr[:], ones[:], lfr[:], 0.0, ALU.mult, ALU.add).then_inc(d_scan, 1)
                        dve.wait_ge(d_scan, b + 1)
                        dve.wait_ge(ds_done, b + 1)
                        dve.tensor_scalar(ncr[:], cr[:], -INV, None, ALU.mult).then_inc(d_ncr, 1)
                        dve.tensor_scalar(cq[:], cr[:, PAST:ALLK], INV, None, ALU.mult).then_inc(d_cq, 1)
                        for e in range(2):
                            ins = dve.tensor_copy(qcols[e * DH:(e + 1) * DH, :, e * DSEQ:(e + 1) * DSEQ],
                                                  qT2[e * DH:(e + 1) * DH, :, ds(b * DSEQ, DSEQ)])
                        ins.then_inc(qbd_done, 1)
                        dve.wait_ge(d_cq, b + 1)
                        dve.wait_ge(d_ncr, b + 1)
                        dve.tensor_tensor(cq_rows[:], same_head[:], cq[:].unsqueeze(1).to_broadcast([H, H, DSEQ]),
                                          ALU.mult).then_inc(d_rows, 1)
                        for p in (0, 2):
                            dve.wait_ge(kT_done, 4 * b + p + 9)
                            dve.tensor_copy(kpT[:, p, :], pK[:, 0, :]).then_inc(kT_copied[0], 1)
                        dve.wait_ge(ds_done, b + 2)
                        dve.tensor_reduce(dmx[0][:], pSS[0:TS, 0:ALLK], AX.X, ALU.max).then_inc(dmx_done, 1)
                        dve.wait_ge(dmx_done, b + 1)
                        dve.tensor_scalar(dmx[1][:], dmx[0][:], -SCALE, None, ALU.mult).then_inc(dnm_done, 1)
                        dve.wait_ge(de_done, b + 2)
                        dve.reciprocal(dmx[3][:], dmx[2][:]).then_inc(dr_done, 1)
                        dve.wait_ge(dr_done, b + 1)
                        dve.wait_ge(dT_done, b + 1)
                        dve.tensor_scalar(prn[0:TS, :], pr[:], dmx[3][:], None, ALU.mult).then_inc(dn_done, 1)
                        dve.wait_ge(dT_done, b + 2)
                        dve.wait_ge(do_copied, b + 1)
                        dve.tensor_copy(prT[:, 0:NPAGES * TS], pP[:, 0:NPAGES * TS])
                        dve.tensor_copy(prT[0:DSEQ, NPAGES * TS:], pP[0:DSEQ, NPAGES * TS:(NPAGES + 1) * TS]
                                        ).then_inc(dT_copied, 1)
                        dve.wait_ge(do_done, b + 3)
                        pairs = pOO[0:DH, 0:TS].rearrange("d (g e q) -> d g e q", e=2, q=DSEQ)
                        for e in range(2):
                            ins = dve.tensor_copy(attnT[e * DH:(e + 1) * DH, :, ds(SEQ + b * DSEQ, DSEQ)],
                                                  pairs[:, :, e, :])
                        ins.then_inc(do_copied, 1)
        late.close()
        attn.close()

        with ExitStack() as ctx:
            mixedT = sb(ctx, "mixedT", [P, KD, T])
            wout = sb(ctx, "wout", [P, KD, D])
            with ExitStack() as inner:
                wg = sb(inner, "wg", [P, 2, 2, KD, P])
                wbr = sb(inner, "wbr", [P, 2, 2, NG, P])
                sg = sb(inner, "sg", [P, 2, 2, 512])
                pG = ps(inner, "pG", [P, 2, 4, 512])

                NC3 = len(COLS)
                wm_in = [sem("wm_in0"), sem("wm_in1")]
                wout_in = sem("wout_in")
                g_done, br_done, sg_done = sem("g_done"), sem("br_done"), sem("sg_done")
                prod_a, prod_b, merged = sem("prod_a"), sem("prod_b"), sem("merged")

                with nc.Block() as block:
                    @block.sync
                    def _(sp):
                        with sp.Fori(0, KD // 2) as i:
                            for par in range(2):
                                n = 2 * i + par
                                sp.wait_ge(br_done, NC3 * n + NC3 - 2 + 2)
                                for j, col in enumerate((GA0, GB0)):
                                    sp.dma_start(wg[:, par, j], win[:, :, ds(n * P + col, P)]).then_inc(wm_in[par], 16)
                                for j, w in enumerate((w_branch_pool, w_branch_attn)):
                                    sp.dma_start(wbr[:, par, j], w[0].rearrange("(c p) n -> p c n", p=P)[:, :, ds(n * P, P)]
                                                 ).then_inc(wm_in[par], 16)

                    @block.gpsimd
                    def _(pool):
                        pool.dma_start(wout[:], w_out[0].rearrange("(c p) n -> p c n", p=P)).then_inc(wout_in, 16)
                        pool.wait_ge(wout_in, 16)

                    @block.tensor
                    def _(pe):
                        pe.sem_inc(br_done, 6)
                        with pe.Fori(0, KD // 2) as i:
                            for par in range(2):
                                pe.wait_ge(wm_in[par], 64 * i + 64)
                                for c, (c0, cn) in enumerate(COLS):
                                    m = NC3 * (2 * i + par) + c
                                    mp = (NC3 * par + c) % 2
                                    pe.wait_ge(merged, m + 1)
                                    for j in range(2):
                                        for d in range(KD):
                                            ins = pe.matmul(pG[:, mp, j, 0:cn], wg[:, par, j, d, :], xnT[:, d, c0:c0 + cn],
                                                            start=(d == 0), stop=(d == KD - 1))
                                        ins.then_inc(g_done, 1)
                                    for j, br in enumerate((poolT, attnT)):
                                        for d in range(NG):
                                            ins = pe.matmul(pG[:, mp, 2 + j, 0:cn], wbr[:, par, j, d, :], br[:, d, c0:c0 + cn],
                                                            start=(d == 0), stop=(d == NG - 1))
                                    ins.then_inc(br_done, 1)

                    @block.scalar
                    def _(act):
                        with act.Fori(0, KD // 2) as i:
                            for mm in range(2 * NC3):
                                m = 2 * NC3 * i + mm
                                cn = COLS[mm % NC3][1]
                                act.wait_ge(merged, m + 1)
                                for j in range(2):
                                    act.wait_ge(g_done, 2 * m + j + 1)
                                    act.activation(sg[:, mm % 2, j, 0:cn], pG[:, mm % 2, j, 0:cn],
                                                   ACT.Sigmoid).then_inc(sg_done, 1)

                    @block.vector
                    def _(dve):
                        dve.sem_inc(merged, 2)
                        with dve.Fori(0, KD // 2) as i:
                            for mm in range(2 * NC3):
                                m = 2 * NC3 * i + mm
                                c0, cn = COLS[mm % NC3]
                                a, b = sg[:, mm % 2, 0, 0:cn], sg[:, mm % 2, 1, 0:cn]
                                dve.wait_ge(br_done, m + 7)
                                dve.wait_ge(sg_done, 2 * m + 2)
                                dve.tensor_tensor(a, a, pG[:, mm % 2, 2, 0:cn], ALU.mult).then_inc(prod_a, 1)
                                dve.tensor_tensor(b, b, pG[:, mm % 2, 3, 0:cn], ALU.mult).then_inc(prod_b, 1)
                                dve.wait_ge(prod_a, m + 1)
                                dve.wait_ge(prod_b, m + 1)
                                dst = mixedT[:, ds(2 * i + mm // NC3, 1), c0:c0 + cn].rearrange("p a t -> p (a t)")
                                dve.tensor_tensor(dst, a, b, ALU.add).then_inc(merged, 1)

            with ExitStack() as inner:
                mx_tile = sb(inner, "mx_tile", [P, 2, KD, P])
                hx = sb(inner, "hx", [P, 2, D])
                hs = sb(inner, "hs", [P, 2, D])
                hnn = sb(inner, "hnn", [P, 2, D])
                hsq = sb(inner, "hsq", [P, D])
                gf = sb(inner, "gf", [P, D])
                hst = [sb(inner, f"hst{i}", [P, 1]) for i in range(4)]
                pHH = ps(inner, "pHH", [P, 2, 1024])

                hx_in = [sem("hx_in0"), sem("hx_in1")]
                gf_in, mt_copied, h_mm, h_add = sem("gf_in"), sem("mt_copied"), sem("h_mm"), sem("h_add")
                h_sq, h_ms, h_sd, h_rs, h_norm = sem("h_sq"), sem("h_ms"), sem("h_sd"), sem("h_rs"), sem("h_norm")
                h_out = [sem("h_out0"), sem("h_out1")]

                with nc.Block() as block:
                    @block.sync
                    def _(sp):
                        def load(t, par, rows):
                            sp.wait_ge(h_add, t + 1)
                            src = xp[ds(t * P, P), :] if rows == P else xs_dram
                            sp.dma_start(hx[0:rows, par, :], src).then_inc(hx_in[par], 16)
                        sp.dma_start(gf[:], norm_ffn_g.to_broadcast([P, D])).then_inc(gf_in, 16)
                        with sp.Fori(0, NT // 2) as i:
                            for par in range(2):
                                load(2 * i + par, par, P)
                        load(NT, 0, TS)

                    @block.gpsimd
                    def _(pool):
                        def copy(t, par, rows):
                            pool.wait_ge(h_mm, t + 1)
                            pool.wait_ge(mt_copied, t + 1)
                            pool.tensor_copy(mx_tile[:, par, :, 0:rows], mixedT[:, :, ds(t * P, rows)]).then_inc(mt_copied, 1)
                        pool.sem_inc(mt_copied, 1)
                        with pool.Fori(0, NT // 2) as i:
                            for par in range(2):
                                copy(2 * i + par, par, P)
                        copy(NT, 0, TS)

                    @block.tensor
                    def _(pe):
                        def tile(t, par, rows):
                            pe.wait_ge(mt_copied, t + 2)
                            pe.wait_ge(h_add, t + 1)
                            for half in range(2):
                                for c in range(KD):
                                    ins = pe.matmul(pHH[0:rows, par, half * 512:(half + 1) * 512],
                                                    mx_tile[:, par, c, 0:rows], wout[:, c, half * 512:(half + 1) * 512],
                                                    start=(c == 0), stop=(c == KD - 1))
                            ins.then_inc(h_mm, 1)
                        pe.sem_inc(h_mm, 2)
                        with pe.Fori(0, NT // 2) as i:
                            for par in range(2):
                                tile(2 * i + par, par, P)
                        tile(NT, 0, TS)

                    @block.scalar
                    def _(act):
                        def tile(t, i, par, rows):
                            act.wait_ge(h_add, t + 3)
                            act.wait_ge(h_sq, t + 1)
                            act.activation(hsq[0:rows, :], hs[0:rows, par, :], ACT.Square,
                                           accum_out=hst[0][0:rows, :]).then_inc(h_sq, 1)
                            act.wait_ge(h_ms, t + 1)
                            act.activation(hst[2][0:rows, :], hst[1][0:rows, :], ACT.Sqrt).then_inc(h_sd, 1)
                            act.wait_ge(h_norm, t + 1)
                            row = ds(t * P, rows)
                            act.dma_start(h_dram[row, :], hs[0:rows, par, :]).then_inc(h_out[par], 16)
                            act.dma_start(hn_dram[row, :], hnn[0:rows, par, :]).then_inc(h_out[par], 16)
                        act.sem_inc(h_sq, 1)
                        with act.Fori(0, NT // 2) as i:
                            for par in range(2):
                                tile(2 * i + par, i, par, P)
                        tile(NT, NT // 2, 0, TS)
                        act.wait_ge(h_out[0], 32 * (NT // 2 + 2))
                        act.wait_ge(h_out[1], 32 * (NT // 2 + 1))

                    @block.vector
                    def _(dve):
                        def tile(t, i, par, rows):
                            dve.wait_ge(h_mm, t + 3)
                            dve.wait_ge(hx_in[par], 16 * i + 16)
                            dve.wait_ge(h_out[par], 32 * i + 32)
                            dve.tensor_tensor(hs[0:rows, par, :], pHH[0:rows, par, :], hx[0:rows, par, :],
                                              ALU.add).then_inc(h_add, 1)
                            dve.wait_ge(h_sq, t + 2)
                            dve.tensor_scalar(hst[1][0:rows, :], hst[0][0:rows, :], 1.0 / D, EPS, ALU.mult,
                                              ALU.add).then_inc(h_ms, 1)
                            dve.wait_ge(h_sd, t + 1)
                            dve.wait_ge(h_norm, t) if isinstance(t, int) else None
                            dve.reciprocal(hst[3][0:rows, :], hst[2][0:rows, :]).then_inc(h_rs, 1)
                            dve.wait_ge(h_rs, t + 1)
                            dve.scalar_tensor_tensor(hnn[0:rows, par, :], hs[0:rows, par, :], hst[3][0:rows, :],
                                                     gf[0:rows, :], ALU.mult, ALU.mult).then_inc(h_norm, 1)
                        dve.sem_inc(h_add, 2)
                        dve.sem_inc(h_out[0], 32)
                        dve.sem_inc(h_out[1], 32)
                        dve.wait_ge(gf_in, 16)
                        with dve.Fori(0, NT // 2) as i:
                            for par in range(2):
                                tile(2 * i + par, i, par, P)
                        tile(NT, NT // 2, 0, TS)
        mid.close()

        RING = 8
        NGP = NPICK // RING
        BOTH = NPC // PH
        HEAD_STEPS, LAST_STEPS = 8, 18
        AHEAD = 2 * RING
        CR = AHEAD + 1
        HALF = NPICK // 2
        CHAIN = PH * HEAD_STEPS + LAST_STEPS
        assert NGP == 16 and PH == 8 and NPICK % RING == 0
        with ExitStack() as ctx:
            wq = sb(ctx, "wq", [P, KD, NPC * P])
            subT = sb(ctx, "subT", [P, NPC, NK])
            ubuf = sb(ctx, "ubuf", [P, RING, D])
            vbuf = sb(ctx, "vbuf", [P, RING, D])
            hn_next = sb(ctx, "hn_next", [P, D])
            hn_cur = sb(ctx, "hn_cur", [P, D])
            h_cur = sb(ctx, "h_cur", [P, D])
            yo = sb(ctx, "yo", [P, D])
            hnT = sb(ctx, "hnT", [P, KD, P])
            qTp = sb(ctx, "qTp", [P, 2, BOTH, P])
            s_sb = sb(ctx, "s_sb", [P, 2, BOTH, NK])
            s_rest = sb(ctx, "s_rest", [P, BOTH, NK])
            v16 = sb(ctx, "v16", [P, NPC, TOPK])
            i16 = sb(ctx, "i16", [P, NPC, TOPK], U32)
            i16f = sb(ctx, "i16f", [P, NPC, TOPK])
            cand = sb(ctx, "cand", [P, TOPK * TOPK])
            cand_rest = sb(ctx, "cand_rest", [P, TOPK * TOPK])
            top_s = sb(ctx, "top_s", [P, PH, TOPK])
            top_p = sb(ctx, "top_p", [P, PH, TOPK], U32)
            part_i = sb(ctx, "part_i", [P, 2, PH, TOPK], U32)
            part_f = sb(ctx, "part_f", [P, 2, PH, TOPK])
            iota16 = sb(ctx, "iota16", [P, TOPK])
            eq = sb(ctx, "eq", [P, PH // 2, TOPK, TOPK])
            half_i = sb(ctx, "half_i", [P, 2, PH, TOPK])
            idx_f = sb(ctx, "idx_f", [P, NPICK])
            idx_next = sb(ctx, "idx_next", [P, NPICK], U32)
            idx_cur = sb(ctx, "idx_cur", [P, NPICK], U32)
            dif = sb(ctx, "dif", [P, PH, TOPK])
            gsum = sb(ctx, "gsum", [P, PH])
            ginv = sb(ctx, "ginv", [P, PH])
            gw_next = sb(ctx, "gw_next", [P, NPICK])
            gw_cur = sb(ctx, "gw_cur", [P, NPICK])
            dots = sb(ctx, "dots", [P, 2, RING])
            gel = sb(ctx, "gel", [P, 2, RING])
            wgt = sb(ctx, "wgt", [P, 2, RING])
            dg = sb(ctx, "dg", [P, RING, P])
            ident2 = sb(ctx, "ident2", [P, TS])
            pA = ps(ctx, "pA", [P, 2, 512])
            pB = ps(ctx, "pB", [P, 2, 512])
            pY = ps(ctx, "pY", [P, 2, 512])

            wq_in, sk_in, skT_done, skT_copied, it_set = (
                sem("wq_in"), sem("sk_in"), sem("skT_done"), sem("skT_copied"), sem("it_set"))
            hn_in, hn_moved, hnT_done, hnT_copied = sem("hn_in"), sem("hn_moved"), sem("hnT_done"), sem("hnT_copied")
            qT_done, qT_copied, sc_done, sc_copied, sc_used = (
                sem("qT_done"), sem("qT_copied"), sem("sc_done"), sem("sc_copied"), sem("sc_used"))
            top_step, dif_done, gexp_done, idx_ready, idx_moved = (
                sem("top_step"), sem("dif_done"), sem("gexp_done"), sem("idx_ready"), sem("idx_moved"))
            gw_moved, i2_set = sem("gw_moved"), sem("i2_set")
            u_in = [sem(f"u_in{s}") for s in range(RING)]
            v_in = [sem(f"v_in{s}") for s in range(RING)]
            u_used, v_used = sem("u_used"), sem("v_used")
            gelu_done, w_done, dg_done = sem("gelu_done"), sem("w_done"), sem("dg_done")
            h_in, h_used, y_copied, y_out = sem("h_in"), sem("h_used"), sem("y_copied"), sem("y_out")

            passed = sem("passed")

            def hold(eng, s, value):
                eng.wait_ge(s, value)
                eng.sem_inc(passed, 1)

            with nc.Block() as block:
                @block.sync
                def _(sp):
                    sp.dma_start(vbuf[:, 0:2, :].rearrange("n a (c k) -> n (a c) k", k=P),
                                 sub_keys[0].rearrange("h p n k -> n (h p) k")).then_inc(sk_in, 16)
                    sp.dma_start(hn_next[:], hn_dram[0:P, :]).then_inc(hn_in, 16)
                    for c in range(4):
                        cols = slice(c * 4 * P, (c + 1) * 4 * P)
                        sp.dma_start(wq[:, :, cols], w_query[0].rearrange("(c p) n -> p c n", p=P)[:, :, cols]
                                     ).then_inc(wq_in, 16)

                    def tile(t, rows, next_rows):
                        sp.wait_ge(h_used, t + 1)
                        sp.dma_start(h_cur[0:rows, :], h_dram[ds(t * P, rows), :]).then_inc(h_in, 16)
                        if next_rows:
                            sp.wait_ge(hn_moved, t + 1)
                            src = hn_dram[ds(t * P + P, next_rows), :]
                            sp.dma_start(hn_next[0:next_rows, :], src).then_inc(hn_in, 16)
                            if next_rows == TS:
                                sp.dma_start(hn_next[TS:P, :], src).then_inc(hn_in, 16)
                        sp.wait_ge(y_copied, t + 2)
                        dst = yp_out[ds(t * P, P), :] if rows == P else ys_out
                        sp.dma_start(dst, yo[0:rows, :]).then_inc(y_out, 16)
                    sp.sem_inc(y_out, 16)
                    with sp.Fori(0, NT - 1) as t:
                        tile(t, P, P)
                    tile(NT - 1, P, TS)
                    tile(NT, TS, 0)
                    sp.wait_ge(y_out, 16 * (NT + 2))

                @block.gpsimd
                def _(pool):
                    pool.iota(iota16[:], pattern=[[1, TOPK]], base=0, channel_multiplier=0,
                              allow_small_or_imprecise_dtypes=True).then_inc(it_set, 1)
                    pool.wait_ge(it_set, 1)

                    def gather(t, k, buf, table, landed, used):
                        s = k % RING
                        hold(pool, used, NPICK * t + k + RING + 2)
                        pool.indirect_dma_start(
                            out=buf[:, s, :], out_offset=None, in_=table[0],
                            in_offset=bass.IndirectOffsetOnAxis(ap=idx_cur[:, k:k + 1], axis=0),
                        ).then_inc(landed[s], 16)

                    def gather_u(t, k):
                        gather(t, k, ubuf, peer_u, u_in, u_used)

                    def gather_v(t, k):
                        gather(t, k, vbuf, peer_v, v_in, v_used)

                    def take_early(t):
                        pool.wait_ge(idx_ready, t + 1)
                        pool.wait_ge(u_used, NPICK * t + 1)
                        hold(pool, v_used, NPICK * t + 1)
                        pool.tensor_copy(idx_cur[:, 0:NPICK - AHEAD], idx_next[:, 0:NPICK - AHEAD]).then_inc(idx_moved, 1)
                        hold(pool, idx_moved, 2 * t + 1)

                    def take_late(t):
                        pool.wait_ge(u_used, NPICK * t + CR)
                        hold(pool, v_used, NPICK * t + CR)
                        pool.tensor_copy(idx_cur[:, NPICK - AHEAD:], idx_next[:, NPICK - AHEAD:]).then_inc(idx_moved, 1)
                        hold(pool, idx_moved, 2 * t + 2)

                    def tile(t, picks, more):
                        for g in range(1, picks // RING):
                            if g == 3 and picks == NPICK:
                                take_late(t)
                            for s in range(RING):
                                gather_u(t, g * RING + s)
                                gather_v(t, (g - 1) * RING + s)
                        if more:
                            take_early(t + 1)
                        for s in range(RING):
                            if more:
                                gather_u(t + 1, s)
                            gather_v(t, picks - RING + s)
                    take_early(0)
                    for s in range(RING):
                        gather_u(0, s)
                    with pool.Fori(0, NT) as t:
                        tile(t, NPICK, True)
                    tile(NT, HALF, False)

                def pe_choose(pe, f, g, rows):
                    if g == 0:
                        pe.wait_ge(hn_in, 16 * f + (16 if rows == P else 32))
                        pe.wait_ge(sc_copied, 8 * f + 2)
                        for j in range(2):
                            for a in range(4):
                                c = 4 * j + a
                                ins = pe.transpose(pA[:, j, a * P:a * P + rows], hn_next[0:rows, c * P:(c + 1) * P],
                                                   ident[0:rows, 0:rows])
                            ins.then_inc(hnT_done, 1)
                    if 2 <= g < 2 + PH:
                        e = g - 2
                        pe.wait_ge(hnT_copied, 2 * f + 2)
                        pe.wait_ge(qT_copied, 8 * f + e + 1)
                        for c in range(BOTH):
                            for d in range(KD):
                                col = (BOTH * e + c) * P
                                ins = pe.matmul(pB[:, e % 2, c * P:c * P + rows], wq[:, d, col:col + P],
                                                hnT[:, d, 0:rows], start=(d == 0), stop=(d == KD - 1))
                        ins.then_inc(qT_done, 1)
                    if 3 <= g < 3 + PH:
                        e = g - 3
                        pe.wait_ge(qT_copied, 8 * f + e + 3)
                        pe.wait_ge(sc_copied, 8 * f + e + 1)
                        for c in range(BOTH):
                            ins = pe.matmul(pA[0:rows, e % 2, c * NK:(c + 1) * NK], qTp[:, e % 2, c, 0:rows],
                                            subT[:, BOTH * e + c, :], start=True, stop=True)
                        ins.then_inc(sc_done, 1)

                def act_choose(act, f, g, rows):
                    if g == 0:
                        for j in range(2):
                            act.wait_ge(hnT_done, 2 * f + j + 1)
                            act.activation(hnT[:, 4 * j:4 * j + 4, 0:rows],
                                           pA[:, j, :].rearrange("p (a b) -> p a b", a=4)[:, :, 0:rows],
                                           ACT.Copy).then_inc(hnT_copied, 1)
                    if 2 <= g < 2 + PH:
                        e = g - 2
                        act.wait_ge(qT_done, 8 * f + e + 1)
                        act.wait_ge(sc_done, 8 * f + e + 1)
                        act.activation(qTp[:, e % 2, :, 0:rows],
                                       pB[:, e % 2, 0:BOTH * P].rearrange("p (a b) -> p a b", a=BOTH)[:, :, 0:rows],
                                       ACT.Copy).then_inc(qT_copied, 1)
                    if 3 <= g < 3 + PH:
                        e = g - 3
                        act.wait_ge(sc_done, 8 * f + e + 3)
                        act.wait_ge(sc_used, 8 * f + e + 1)
                        act.activation(s_sb[0:rows, e % 2].rearrange("p a b -> p (a b)"),
                                       pA[0:rows, e % 2, 0:BOTH * NK], ACT.Copy).then_inc(sc_copied, 1)
                    if g == 13:
                        act.wait_ge(dif_done, f + 1)
                        act.activation(dif[0:rows], dif[0:rows], ACT.Exp).then_inc(gexp_done, 1)

                def dve_choose(dve, f, g, rows, count):
                    def step(ins):
                        count[0] += 1
                        ins.then_inc(top_step, 1)
                        hold(dve, top_step, CHAIN * f + count[0])

                    R = slice(0, rows)
                    first = isinstance(f, int) and f == 0
                    packed = [(0, slice(0, NPICK))] if rows == P else [(0, slice(0, HALF)), (TS, slice(HALF, NPICK))]
                    if 4 <= g < 4 + PH:
                        e = g - 4
                        hold(dve, sc_copied, 8 * f + e + 3)
                        sides = [(c, s_sb[R, e % 2, c, :], s_rest[R, c, :], BOTH * e + c) for c in range(BOTH)]
                        for c, s, rest, n in sides:
                            ins = dve.max(v16[R, n, 0:8], s)
                        step(ins)
                        for c, s, rest, n in sides:
                            dve.max_index(i16[R, n, 0:8], v16[R, n, 0:8], s)
                            ins = dve.match_replace(rest, v16[R, n, 0:8], s, LOWEST)
                        step(ins)
                        for c, s, rest, n in sides:
                            ins = dve.max(v16[R, n, 8:16], rest)
                        step(ins)
                        for c, s, rest, n in sides:
                            ins = dve.max_index(i16[R, n, 8:16], v16[R, n, 8:16], rest)
                        ins.then_inc(sc_used, 1)
                        step(dve.tensor_tensor(cand[R, :].rearrange("p (a b) -> p a b", a=TOPK),
                                               v16[R, 2 * e, :].unsqueeze(2).to_broadcast([rows, TOPK, TOPK]),
                                               v16[R, 2 * e + 1, :].unsqueeze(1).to_broadcast([rows, TOPK, TOPK]), ALU.add))
                        step(dve.max(top_s[R, e, 0:8], cand[R, :]))
                        dve.max_index(top_p[R, e, 0:8], top_s[R, e, 0:8], cand[R, :])
                        step(dve.match_replace(cand_rest[R, :], top_s[R, e, 0:8], cand[R, :], LOWEST))
                        step(dve.max(top_s[R, e, 8:16], cand_rest[R, :]))
                        step(dve.max_index(top_p[R, e, 8:16], top_s[R, e, 8:16], cand_rest[R, :]))
                    if g == 12:
                        dve.tensor_tensor(dif[R], top_s[R], top_s[R, :, 0:1].to_broadcast([rows, PH, TOPK]),
                                          ALU.subtract).then_inc(dif_done, 1)
                        dve.tensor_scalar(part_i[R, 0], top_p[R], 4, None, ALU.logical_shift_right)
                        dve.tensor_copy(i16f[R], i16[R])
                        step(dve.tensor_scalar(part_i[R, 1], top_p[R], TOPK - 1, None, ALU.bitwise_and))
                        step(dve.tensor_copy(part_f[R], part_i[R]))
                    if g >= 12:
                        side, half = divmod(g - 12, 2)
                        hs_ = slice(half * PH // 2, (half + 1) * PH // 2)
                        numbers = i16f[R].rearrange("p (h c) k -> p c h k", c=2)[:, side, hs_, :]
                        shape = [rows, PH // 2, TOPK, TOPK]
                        step(dve.tensor_tensor(eq[R], part_f[R, side, hs_, :].unsqueeze(3).to_broadcast(shape),
                                               iota16[R].unsqueeze(1).unsqueeze(1).to_broadcast(shape), ALU.is_equal))
                        step(dve.tensor_tensor(eq[R], eq[R], numbers.unsqueeze(2).to_broadcast(shape), ALU.mult))
                        step(dve.tensor_reduce(half_i[R, side, hs_, :], eq[R], AX.X, ALU.add))
                    if g == 14:
                        dve.wait_ge(gexp_done, f + 1)
                        step(dve.tensor_reduce(gsum[R], dif[R], AX.X, ALU.add))
                        step(dve.reciprocal(ginv[R], gsum[R]))
                        if not first:
                            dve.wait_ge(gw_moved, f)
                        for r0, picks in packed:
                            hh = slice(picks.start // TOPK, picks.stop // TOPK)
                            ins = dve.tensor_tensor(
                                gw_next[r0:r0 + rows, 0:picks.stop - picks.start].rearrange("p (h k) -> p h k", k=TOPK),
                                dif[R, hh], ginv[R, hh].unsqueeze(2).to_broadcast([rows, hh.stop - hh.start, TOPK]), ALU.mult)
                        step(ins)
                    if g == 15:
                        step(dve.scalar_tensor_tensor(idx_f[R], half_i[R, 0].rearrange("p h k -> p (h k)"), float(NK),
                                                      half_i[R, 1].rearrange("p h k -> p (h k)"), ALU.mult, ALU.add))
                        if not first:
                            dve.wait_ge(idx_moved, 2 * f)
                        for r0, picks in packed:
                            ins = dve.tensor_copy(idx_next[r0:r0 + rows, 0:picks.stop - picks.start], idx_f[R, picks])
                        ins.then_inc(idx_ready, 1)
                        assert count[0] == CHAIN, count

                @block.tensor
                def _(pe):
                    pe.wait_ge(sk_in, 16)
                    for c in range(4):
                        if c >= 2:
                            pe.wait_ge(skT_copied, c - 1)
                        for a in range(4):
                            n = 4 * c + a
                            ins = pe.transpose(pB[:, c % 2, a * P:(a + 1) * P],
                                               vbuf[:, n // 8, (n % 8) * P:(n % 8 + 1) * P], ident[:])
                        ins.then_inc(skT_done, 1)
                    pe.wait_ge(wq_in, 64)
                    pe.wait_ge(skT_copied, 4)
                    pe.sem_inc(v_used, CR)
                    pe.sem_inc(h_used, 1)
                    pe.sem_inc(sc_done, 2)
                    for g in range(NGP):
                        pe_choose(pe, 0, g, P)

                    def weigh(t, g, picks, rows):
                        for s in range(RING):
                            k = g * RING + s
                            pe.wait_ge(v_in[s], 16 * (NGP * t + g + 1))
                            pe.wait_ge(dg_done, NPICK * t + k + 1)
                            for half in range(2):
                                ins = pe.matmul(pY[0:rows, half, :], dg[:, s, 0:rows],
                                                vbuf[:, s, half * 512:(half + 1) * 512],
                                                start=False, stop=(k == picks - 1))
                            ins.then_inc(v_used, 1)

                    def tile(t, picks, rows, next_rows):
                        for g in range(picks // RING):
                            if g == 1:
                                pe.wait_ge(h_in, 16 * t + 16)
                                pe.wait_ge(y_copied, t + 1)
                                for half in range(2):
                                    ins = pe.matmul(pY[0:rows, half, :], ident[0:rows, 0:rows],
                                                    h_cur[0:rows, half * 512:(half + 1) * 512], start=True, stop=False)
                                ins.then_inc(h_used, 1)
                            if g:
                                weigh(t, g - 1, picks, rows)
                            if next_rows:
                                pe_choose(pe, t + 1, g, next_rows)
                        weigh(t, picks // RING - 1, picks, rows)
                    with pe.Fori(0, NT - 1) as t:
                        tile(t, NPICK, P, P)
                    tile(NT - 1, NPICK, P, TS)
                    tile(NT, HALF, TS, 0)

                @block.scalar
                def _(act):
                    act.sem_inc(qT_copied, 2)
                    act.sem_inc(sc_copied, 2)
                    for c in range(4):
                        act.wait_ge(skT_done, c + 1)
                        act.activation(subT[:, 4 * c:4 * c + 4, :], pB[:, c % 2, :].rearrange("p (a b) -> p a b", a=4),
                                       ACT.Copy).then_inc(skT_copied, 1)
                    for e in range(2):
                        ins = act.activation(ident2[e * TS:(e + 1) * TS, :], ident[e * TS:(e + 1) * TS, e * TS:(e + 1) * TS],
                                             ACT.Copy)
                    ins.then_inc(i2_set, 1)
                    act.wait_ge(i2_set, 1)
                    act.sem_inc(y_copied, 1)
                    for g in range(NGP):
                        act_choose(act, 0, g, P)

                    def diagonals(t, g, rows):
                        act.wait_ge(w_done, NGP * t + g + 1)
                        eye = ident if rows == P else ident2
                        for s in range(RING):
                            act.wait_ge(v_used, NPICK * t + g * RING + s + RING + 2)
                            act.activation(dg[:, s, 0:rows], eye[:, 0:rows], ACT.Copy,
                                           scale=wgt[:, g % 2, s:s + 1]).then_inc(dg_done, 1)

                    def tile(t, picks, rows, next_rows):
                        for g in range(picks // RING):
                            if g:
                                diagonals(t, g - 1, rows)
                            if next_rows:
                                act_choose(act, t + 1, g, next_rows)
                            act.wait_ge(u_used, NPICK * t + (g + 1) * RING + CR)
                            act.activation(gel[:, g % 2, :], dots[:, g % 2, :], ACT.Gelu).then_inc(gelu_done, 1)
                        diagonals(t, picks // RING - 1, rows)
                        act.wait_ge(v_used, NPICK * t + picks + CR)
                        act.wait_ge(y_out, 16 * t + 16)
                        act.activation(yo[0:rows, :], pY[0:rows].rearrange("p a b -> p (a b)"),
                                       ACT.Copy).then_inc(y_copied, 1)
                    with act.Fori(0, NT - 1) as t:
                        tile(t, NPICK, P, P)
                    tile(NT - 1, NPICK, P, TS)
                    tile(NT, HALF, TS, 0)

                @block.vector
                def _(dve):
                    dve.sem_inc(u_used, CR)
                    dve.sem_inc(sc_used, 2)
                    dve.wait_ge(it_set, 1)
                    count = [0]
                    for g in range(NGP):
                        dve_choose(dve, 0, g, P, count)

                    def weights(t, g):
                        dve.wait_ge(gelu_done, NGP * t + g + 1)
                        dve.tensor_tensor(wgt[:, g % 2, :], gel[:, g % 2, :],
                                          gw_cur[:, g * RING:(g + 1) * RING], ALU.mult).then_inc(w_done, 1)

                    def tile(t, picks, next_rows):
                        count = [0]
                        dve.wait_ge(idx_ready, t + 1)
                        if picks == HALF:
                            dve.wait_ge(hn_in, 16 * t + 32)
                        dve.wait_ge(u_used, NPICK * t + CR)
                        dve.tensor_copy(hn_cur[:], hn_next[:]).then_inc(hn_moved, 1)
                        dve.tensor_copy(gw_cur[:, 0:picks], gw_next[:, 0:picks]).then_inc(gw_moved, 1)
                        dve.wait_ge(hn_moved, t + 1)
                        dve.wait_ge(gw_moved, t + 1)
                        for g in range(picks // RING):
                            for s in range(RING):
                                if g and s == 3:
                                    weights(t, g - 1)
                                dve.wait_ge(u_in[s], 16 * (NGP * t + g + 1))
                                dve.tensor_tensor_reduce(ubuf[:, s, :], ubuf[:, s, :], hn_cur[:], 1.0, 0.0,
                                                         ALU.mult, ALU.add, dots[:, g % 2, s:s + 1]).then_inc(u_used, 1)
                            if next_rows:
                                dve_choose(dve, t + 1, g, next_rows, count)
                        weights(t, picks // RING - 1)
                        dve.wait_ge(w_done, NGP * t + picks // RING)
                    with dve.Fori(0, NT - 1) as t:
                        tile(t, NPICK, P)
                    tile(NT - 1, NPICK, TS)
                    tile(NT, HALF, 0)


_INS = ['x_prompt', 'x_sample', 'cache_k', 'cache_v', 'cache_logf', 'state_pool', 'page_table', 'norm_mix_g',
        'w_in', 'b_forget', 'q_norm_g', 'k_norm_g', 'pool_mix_w', 'pool_scale', 'w_branch_pool',
        'w_branch_attn', 'w_out', 'norm_ffn_g', 'w_query', 'sub_keys', 'peer_u', 'peer_v']


def kernel(**inputs):
    import numpy as _np
    import concourse.bacc as _bacc
    from concourse import mybir as _mybir
    from concourse.bass_utils import run_bass_kernel_spmd as _run

    arrays, args = {}, []
    nc = _bacc.Bacc("TRN2", target_bir_lowering=False, num_devices=1)
    for name in _INS:
        a = _np.ascontiguousarray(inputs[name])
        arrays[f"in_{name}_dram"] = a
        args.append(nc.dram_tensor(f"in_{name}_dram", a.shape, _mybir.dt.from_np(a.dtype), kind="ExternalInput").ap())
    x_prompt, x_sample = inputs['x_prompt'], inputs['x_sample']
    batch, seq = x_prompt.shape[:2]
    dec, dseq = x_sample.shape[:2]
    depth, _, _, heads, dim = inputs['cache_k'].shape
    hist, dpool = inputs['state_pool'].shape[2:]
    outs = [x_prompt.shape, x_sample.shape,
            (depth, batch, seq, heads, dim), (depth, batch, seq, heads, dim), (depth, batch, seq, heads),
            (depth, batch, hist, dpool),
            (depth, dec, dseq, heads, dim), (depth, dec, dseq, heads, dim), (depth, dec, dseq, heads),
            (depth, dec, hist, dpool)]
    for i, shape in enumerate(outs):
        args.append(nc.dram_tensor(f"out_{i}_dram", tuple(shape), _mybir.dt.float32, kind="ExternalOutput").ap())
    build(nc, *args)
    r = _run(nc, [arrays], core_ids=[0])
    return tuple(r.results[0][f"out_{i}_dram"] for i in range(len(outs)))
```

```python
from contextlib import ExitStack

import concourse.bass as bass
from concourse import mybir

F32 = mybir.dt.float32
BF16 = mybir.dt.bfloat16
U32 = mybir.dt.uint32
I32 = mybir.dt.int32
ALU = mybir.AluOpType
ACT = mybir.ActivationFunctionType
AX = mybir.AxisListType
ds = bass.ds

P = 128
EPS = 1e-6
NEG = -1.0e30
LOWEST = -3.0e38
POOL_WINDOWS = (2, 4, 8, 16)


def build(nc, x_prompt, x_sample, cache_k, cache_v, cache_logf, state_pool, page_table, norm_mix_g, w_in,
          b_forget, q_norm_g, k_norm_g, pool_mix_w, pool_scale, w_branch_pool, w_branch_attn, w_out,
          norm_ffn_g, w_query, sub_keys, peer_u, peer_v,
          y_prompt, y_sample, k_prompt, v_prompt, logf_prompt, pool_prompt,
          k_sample, v_sample, logf_sample, pool_sample):
    _, SEQ, D = x_prompt.shape
    NSEQ, DSEQ, _ = x_sample.shape
    _, NPHYS, PAGE, H, DH = cache_k.shape
    NPAGES = page_table.shape[1]
    HIST = state_pool.shape[2]
    DA = H * DH
    DP = state_pool.shape[3]
    KD = D // P
    NG = DP // P
    TS = NSEQ * DSEQ
    T = SEQ + TS
    NT = SEQ // P
    PAST = NPAGES * PAGE
    ALLK = PAST + DSEQ
    PH = sub_keys.shape[1]
    NK = sub_keys.shape[3]
    TOPK = 16
    NPICK = PH * TOPK
    NPC = PH * 2
    SCALE = float(DH) ** -0.5
    INV = 1.0 / SCALE
    RING = 8
    COLS = [(0, 512), (512, 512), (SEQ, TS)]
    QKV0 = DP
    F0 = DP + 3 * DA
    GA0 = F0 + H
    GB0 = GA0 + D
    assert P == PAGE and DH * 2 == P and PAST == 512 and SEQ == 1024 and NK == P

    xp = x_prompt.rearrange("a t d -> (a t) d")
    xs_dram = x_sample.rearrange("b t d -> (b t) d")
    kp_out = k_prompt.rearrange("l a t h d -> (l a t) (h d)")
    vp_out = v_prompt.rearrange("l a t h d -> (l a t) (h d)")
    ks_out = k_sample.rearrange("l b t h d -> (l b t) (h d)")
    vs_out = v_sample.rearrange("l b t h d -> (l b t) (h d)")
    lfp_out = logf_prompt.rearrange("l a (n p) h -> p (l a n) h", p=P)
    lfs_out = logf_sample.rearrange("l b t h -> (l b t) h")
    yp_out = y_prompt.rearrange("a t d -> (a t) d")
    ys_out = y_sample.rearrange("b t d -> (b t) d")
    win = w_in[0].rearrange("(c p) n -> p c n", p=P)
    ck = cache_k[0].rearrange("n t h d -> n t (h d)")
    cv = cache_v[0].rearrange("n t h d -> n t (h d)")
    clf = cache_logf[0]
    h_dram = nc.dram_tensor("h_scratch", [T, D], F32, kind="Internal").ap()
    hn_dram = nc.dram_tensor("hn_scratch", [T, D], F32, kind="Internal").ap()

    with ExitStack() as top:
        def sb(ctx, name, shape, dt=F32):
            return ctx.enter_context(nc.sbuf_tensor(name, shape, dt))

        def ps(ctx, name, shape, dt=F32):
            return ctx.enter_context(nc.psum_tensor(name, shape, dt))

        in_use, spare = [], []

        def sem(name):
            if spare:
                return spare.pop(0)
            in_use.append(top.enter_context(nc.semaphore(name)))
            return in_use[-1]

        passed = top.enter_context(nc.semaphore("passed"))

        def hold(eng, s, value):
            eng.wait_ge(s, value)
            eng.sem_inc(passed, 1)

        ident = sb(top, "ident", [P, P])
        identb = sb(top, "identb", [P, P], BF16)

        causal = sb(top, "causal", [P, P], BF16)
        causal8 = sb(top, "causal8", [DSEQ, DSEQ], BF16)
        rep_q = sb(top, "rep_q", [DSEQ, H, DSEQ], BF16)
        same_head = sb(top, "same_head", [H, H, DSEQ])
        causalT = sb(top, "causalT", [P, P], BF16)
        rcnt = sb(top, "rcnt", [P, 16])

        c_set, c_sel, c_dve, c_iota = sem("c_set"), sem("c_sel"), sem("c_dve"), sem("c_iota")
        with nc.Block() as block:
            @block.gpsimd
            def _(pool):
                pool.memset(ident[:], 0.0).then_inc(c_set, 1)
                pool.memset(identb[:], 0.0).then_inc(c_set, 1)
                pool.memset(causal[:], 0.0).then_inc(c_set, 1)
                pool.memset(causal8[:], 0.0).then_inc(c_set, 1)
                pool.memset(rep_q[:], 0.0).then_inc(c_set, 1)
                pool.memset(same_head[:], 0.0).then_inc(c_set, 1)
                pool.memset(causalT[:], 0.0).then_inc(c_set, 1)
                pool.wait_ge(c_set, 7)
                for m in (ident, identb):
                    pool.affine_select(out=m[:], in_=m[:], compare_op=ALU.not_equal, fill=1.0, base=0,
                                       pattern=[[-1, P]], channel_multiplier=1).then_inc(c_sel, 1)
                for m, n in ((causal, P), (causal8, DSEQ)):
                    pool.affine_select(out=m[:], in_=m[:], compare_op=ALU.is_ge, fill=NEG, base=0,
                                       pattern=[[-1, n]], channel_multiplier=1).then_inc(c_sel, 1)
                pool.affine_select(out=causalT[:], in_=causalT[:], compare_op=ALU.is_ge, fill=NEG, base=0,
                                   pattern=[[1, P]], channel_multiplier=-1).then_inc(c_sel, 1)
                pool.affine_select(out=rep_q[:], in_=rep_q[:], compare_op=ALU.not_equal, fill=1.0, base=0,
                                   pattern=[[0, H], [-1, DSEQ]], channel_multiplier=1).then_inc(c_sel, 1)
                pool.affine_select(out=same_head[:], in_=same_head[:], compare_op=ALU.not_equal, fill=1.0,
                                   base=0, pattern=[[-1, H], [0, DSEQ]], channel_multiplier=1).then_inc(c_sel, 1)
                pool.iota(rcnt[:], pattern=[[1, 16]], base=1, channel_multiplier=0,
                          allow_small_or_imprecise_dtypes=True).then_inc(c_iota, 1)
                pool.wait_ge(c_sel, 7)

            @block.vector
            def _(dve):
                dve.wait_ge(c_iota, 1)
                dve.reciprocal(rcnt[:], rcnt[:]).then_inc(c_dve, 1)
                dve.wait_ge(c_dve, 1)

        inputs = sb(top, "inputs", [P, 2 * KD * T])
        xnT = inputs[:, 0:KD * T].rearrange("p (c t) -> p c t", c=KD)
        branch = inputs[:, KD * T:]
        poolT = branch[:, 0:NG * T].rearrange("p (g t) -> p g t", g=NG)
        attnT = branch[:, NG * T:].rearrange("p (g t) -> p g t", g=NG)
        work = sb(top, "work", [P, (2 * RING + 1) * D])
        pages = sb(top, "pages", [1, NSEQ * NPAGES], I32)
        attn = top.enter_context(ExitStack())
        heads = work[:, 0:2 * H * SEQ]
        qT, kT = (heads[0:DH + 3, j * H * SEQ:(j + 1) * H * SEQ].rearrange("p (h t) -> p h t", h=H) for j in range(2))
        v_sb = sb(attn, "v_sb", [P, NT + 1, DA])
        qT2 = sb(attn, "qT2", [P, NG, TS])
        kT2 = sb(attn, "kT2", [P, NG, TS])

        front = attn.enter_context(ExitStack())
        wf = sb(attn, "wf", [P, KD, H])
        pFX = ps(front, "pFX", [P, 512])
        f_logits = pFX[:, P:P + (NT + 1) * H]
        wu0 = work[:, 2 * H * SEQ:2 * H * SEQ + KD * P].rearrange("p (c n) -> p c n", c=KD)
        with ExitStack() as ctx:
            wqkv = sb(ctx, "wqkv", [P, KD, 3 * DA])
            xb = branch[:, 0:2 * D].rearrange("p (a n) -> p a n", a=2)
            xsc = branch[:, 2 * D:3 * D]
            sqx = branch[:, 3 * D:4 * D]
            xnc = xb.rearrange("p a (c n) -> p a c n", c=KD)
            qk = branch[:, 4 * D:6 * D].rearrange("p (a n) -> p a n", a=2)
            gqk = sb(ctx, "gqk", [P, 2, DH])
            gx = sb(ctx, "gx", [P, KD])
            stx = [sb(ctx, f"stx{i}", [P, 1]) for i in range(4)]
            stq = [sb(ctx, f"stq{i}", [P, 2 * H]) for i in range(4)]
            pT = ps(ctx, "pT", [P, 2, 512])
            pQK = ps(ctx, "pQK", [P, 2, 512])
            pV = ps(ctx, "pV", [P, 512])
            pH = ps(ctx, "pH", [P, 2, 512])

            x_in = [sem("x_in0"), sem("x_in1")]
            w_q_in, w_k_in, w_v_in, gain_in = sem("w_q_in"), sem("w_k_in"), sem("w_v_in"), sem("gain_in")
            sq_done, ms_done, sd_done = sem("sq_done"), sem("ms_done"), sem("sd_done")
            rs_done, xs_done, xT_done = sem("rs_done"), sem("xs_done"), sem("xT_done")
            xnc_done, xnT_done = sem("xnc_done"), sem("xnT_done")
            q_done, k_done, v_done = sem("q_done"), sem("k_done"), sem("v_done")
            sqqk_done, ssq_done, msq_done, sdq_done, rsq_done = (
                sem("sqqk_done"), sem("ssq_done"), sem("msq_done"), sem("sdq_done"), sem("rsq_done"))
            qkn_done, qg_done, qkg_done = sem("qkn_done"), sem("qg_done"), sem("qkg_done")
            hT_done, hT_copied, v_copied = sem("hT_done"), sem("hT_copied"), sem("v_copied")
            kv_out = [sem("kv_out0"), sem("kv_out1")]
            wf_in, wu0_in = sem("wf_in"), sem("wu0_in")
            kv_out_s, aug_set = sem("kv_out_s"), sem("aug_set")

            def in_pairs(eng, tile):
                with eng.Fori(0, NT // 2 - 1) as i:
                    for par in range(2):
                        tile(i * 2 + par, i, par, P, P)
                tile(NT - 2, NT // 2 - 1, 0, P, P)
                tile(NT - 1, NT // 2 - 1, 1, P, TS)
                tile(NT, NT // 2, 0, TS, 0)

            with nc.Block() as block:
                @block.sync
                def _(sp):
                    def load_x(t, i, par, rows):
                        sp.wait_ge(v_done, t + 1)
                        sp.wait_ge(xnT_done, t + 1)
                        src = xp[ds(t * P, rows), :] if rows == P else xs_dram
                        sp.dma_start(xb[0:rows, par, :], src).then_inc(x_in[par], 16)
                    sp.sem_inc(kv_out[0], 32)
                    sp.sem_inc(kv_out[1], 32)
                    load_x(0, 0, 0, P)
                    sp.dma_start(gqk[:, 0, :], q_norm_g.to_broadcast([P, DH])).then_inc(gain_in, 16)
                    sp.dma_start(gqk[:, 1, :], k_norm_g.to_broadcast([P, DH])).then_inc(gain_in, 16)
                    with nc.allow_non_contiguous_dma(reason="a gain per partition, once"):
                        sp.dma_start(gx[:], norm_mix_g[0].rearrange("(c p) -> p c", p=P)).then_inc(gain_in, 16)
                        sp.dma_start(wf[:], win[:, :, F0:F0 + H]).then_inc(wf_in, 16)
                    sp.dma_start(pages[:], page_table.rearrange("b n -> (b n)").unsqueeze(0)).then_inc(gain_in, 16)
                    load_x(1, 0, 1, P)
                    sp.dma_start(wu0, win[:, :, 0:P]).then_inc(wu0_in, 16)
                    with sp.Fori(1, NT // 2) as i:
                        for par in range(2):
                            load_x(i * 2 + par, i, par, P)
                    load_x(NT, NT // 2, 0, TS)
                    sp.wait_ge(wu0_in, 16)

                @block.gpsimd
                def _(pool):
                    pool.sem_inc(xnT_done, 2)
                    for c, s in enumerate((w_q_in, w_k_in, w_v_in)):
                        pool.dma_start(wqkv[:, :, c * DA:(c + 1) * DA],
                                       win[:, :, QKV0 + c * DA:QKV0 + (c + 1) * DA]).then_inc(s, 16)
                    pool.memset(qT[DH:, :, :], 1.0).then_inc(aug_set, 1)
                    pool.wait_ge(aug_set, 1)
                    pool.memset(kT[DH:, :, :], 1.0).then_inc(aug_set, 1)
                    pool.wait_ge(aug_set, 2)

                    def keep_xn(t, par, rows):
                        pool.wait_ge(xnT_done, t + 2)
                        pool.wait_ge(xnc_done, 2 * t + 4)
                        pool.tensor_copy(xnT[:, :, ds(t * P, rows)], xnc[:, par, :, 0:rows]).then_inc(xnT_done, 1)
                    with pool.Fori(0, NT // 2) as i:
                        for par in range(2):
                            keep_xn(i * 2 + par, par, P)
                    keep_xn(NT, 0, TS)
                    pool.wait_ge(xnT_done, NT + 3)

                @block.scalar
                def _(act):
                    def x_norm(t, i, par, rows):
                        act.wait_ge(x_in[par], 16 * (i + 1))
                        act.wait_ge(ssq_done, t + 1)
                        act.activation(sqx[0:rows, :], xb[0:rows, par, :], ACT.Square,
                                       accum_out=stx[0][0:rows, :]).then_inc(sq_done, 1)
                        act.wait_ge(ms_done, t + 1)
                        act.activation(stx[2][0:rows, :], stx[1][0:rows, :], ACT.Sqrt).then_inc(sd_done, 1)

                    def tile(t, i, par, rows, next_rows):
                        last = rows != P
                        if next_rows:
                            x_norm(t + 1, i + par, 1 - par, next_rows)
                        act.wait_ge(q_done, t + 1)
                        act.wait_ge(k_done, t + 1)
                        act.wait_ge(sq_done, t + (2 if next_rows else 1))
                        act.wait_ge(ssq_done, t + 2)
                        act.activation(sqx[0:rows, :], pQK[0:rows, :, :].rearrange("p a b -> p (a b)"),
                                       ACT.Square).then_inc(sqqk_done, 1)
                        act.wait_ge(msq_done, t + 1)
                        act.activation(stq[1][0:rows, :], stq[0][0:rows, :], ACT.Sqrt).then_inc(sdq_done, 1)
                        act.wait_ge(v_done, t + 3)
                        v_tile = v_sb[0:rows, NT, :] if last else v_sb[:, ds(t, 1), :].rearrange("p a b -> p (a b)")
                        act.activation(v_tile, pV[0:rows, :], ACT.Copy).then_inc(v_copied, 1)
                        act.wait_ge(v_copied, t + 2)
                        act.wait_ge(qkg_done, t + 1)
                        if last:
                            act.dma_start(ks_out, qk[0:rows, par, DA:]).then_inc(kv_out_s, 16)
                            act.dma_start(vs_out, v_tile).then_inc(kv_out_s, 16)
                            for j, dst in enumerate((qT2, kT2)):
                                act.wait_ge(hT_done, 2 * NT + j + 5)
                                act.activation(dst[:], pH[:, j, 0:NG * TS].rearrange("p (a b) -> p a b", a=NG),
                                               ACT.Copy).then_inc(hT_copied, 1)
                            act.wait_ge(hT_copied, 4 * NT + 6)
                        else:
                            act.dma_start(kp_out[ds(t * P, P), :], qk[:, par, DA:]).then_inc(kv_out[par], 16)
                            act.dma_start(vp_out[ds(t * P, P), :], v_tile).then_inc(kv_out[par], 16)
                            for j, dst in enumerate((qT, kT)):
                                act.wait_ge(hT_done, 2 * t + j + 5)
                                for e in range(2):
                                    act.activation(dst[0:DH, e:H:2, ds(t * P, P)],
                                                   pH[e * DH:(e + 1) * DH, j, :].rearrange("p (a b) -> p a b", a=4),
                                                   ACT.Copy).then_inc(hT_copied, 1)
                    act.sem_inc(hT_copied, 4)
                    act.sem_inc(v_copied, 1)
                    x_norm(0, 0, 0, P)
                    in_pairs(act, tile)
                    act.wait_ge(kv_out[0], 32 * (NT // 2 + 1))
                    act.wait_ge(kv_out[1], 32 * (NT // 2 + 1))
                    act.wait_ge(kv_out_s, 32)

                @block.vector
                def _(dve):
                    def x_scale(t, par, rows):
                        dve.wait_ge(sq_done, t + 1)
                        dve.tensor_scalar(stx[1][0:rows, :], stx[0][0:rows, :], 1.0 / D, EPS, ALU.mult,
                                          ALU.add).then_inc(ms_done, 1)
                        dve.wait_ge(sd_done, t + 1)
                        dve.reciprocal(stx[3][0:rows, :], stx[2][0:rows, :]).then_inc(rs_done, 1)
                        dve.wait_ge(rs_done, t + 1)
                        dve.wait_ge(xT_done, 2 * t + 2)
                        dve.tensor_scalar(xsc[0:rows, :], xb[0:rows, par, :], stx[3][0:rows, :], None,
                                          ALU.mult).then_inc(xs_done, 1)

                    def x_gain(t, par, rows):
                        dve.wait_ge(xs_done, t + 1)
                        for j in range(2):
                            dve.wait_ge(xT_done, 2 * t + j + 3)
                            dve.tensor_tensor(xnc[:, par, 4 * j:4 * j + 4, 0:rows],
                                              pT[:, j, :].rearrange("p (a b) -> p a b", a=4)[:, :, 0:rows],
                                              gx[:, 4 * j:4 * j + 4].unsqueeze(2).to_broadcast([P, 4, rows]),
                                              ALU.mult).then_inc(xnc_done, 1)

                    def tile(t, i, par, rows, next_rows):
                        if next_rows:
                            x_scale(t + 1, 1 - par, next_rows)
                        dve.wait_ge(sqqk_done, t + 1)
                        dve.tensor_reduce(stq[2][0:rows, :], sqx[0:rows, :].rearrange("p (h d) -> p h d", d=DH),
                                          AX.X, ALU.add).then_inc(ssq_done, 1)
                        dve.wait_ge(ssq_done, t + 3)
                        dve.tensor_scalar(stq[0][0:rows, :], stq[2][0:rows, :], 1.0 / DH, EPS, ALU.mult,
                                          ALU.add).then_inc(msq_done, 1)
                        if next_rows:
                            x_gain(t + 1, 1 - par, next_rows)
                        dve.wait_ge(sdq_done, t + 1)
                        dve.reciprocal(stq[3][0:rows, :], stq[1][0:rows, :]).then_inc(rsq_done, 1)
                        dve.wait_ge(rsq_done, t + 1)
                        dve.wait_ge(kv_out[par], 32 * i + 32)
                        dve.wait_ge(hT_done, 2 * t + 2)
                        dve.tensor_tensor(qk[0:rows, par, :].rearrange("p (h d) -> p h d", d=DH),
                                          pQK[0:rows, :, :].rearrange("p a (h d) -> p (a h) d", d=DH),
                                          stq[3][0:rows, :].unsqueeze(2).to_broadcast([rows, 2 * H, DH]),
                                          ALU.mult).then_inc(qkn_done, 1)
                        dve.wait_ge(qkn_done, t + 2)
                        for j, s in enumerate((qg_done, qkg_done)):
                            half = qk[0:rows, par, j * DA:(j + 1) * DA].rearrange("p (h d) -> p h d", d=DH)
                            dve.tensor_tensor(half, half, gqk[0:rows, j, :].unsqueeze(1).to_broadcast([rows, H, DH]),
                                              ALU.mult).then_inc(s, 1)
                    dve.sem_inc(xnc_done, 2)
                    dve.sem_inc(qkn_done, 1)
                    dve.sem_inc(ssq_done, 2)
                    dve.wait_ge(gain_in, 64)
                    x_scale(0, 0, P)
                    x_gain(0, 0, P)
                    in_pairs(dve, tile)

                @block.tensor
                def _(pe):
                    def turn_x(t, rows):
                        pe.wait_ge(xs_done, t + 1)
                        for j in range(2):
                            pe.wait_ge(xnc_done, 2 * t + j + 1)
                            for a in range(4):
                                c = 4 * j + a
                                ins = pe.transpose(pT[:, j, a * P:a * P + rows], xsc[0:rows, c * P:(c + 1) * P],
                                                   ident[0:rows, 0:rows])
                            ins.then_inc(xT_done, 1)

                    def tile(t, i, par, rows, next_rows):
                        pe.wait_ge(xnc_done, 2 * t + 4)
                        for n, (out, w_in_sem, done) in enumerate(((pQK[0:rows, 0, :], w_q_in, q_done),
                                                                   (pQK[0:rows, 1, :], w_k_in, k_done),
                                                                   (pV[0:rows, :], w_v_in, v_done))):
                            if n == 2:
                                pe.wait_ge(wf_in, 16)
                                for c in range(KD):
                                    pe.matmul(f_logits[0:rows, ds(t * H, H)], xnc[:, par, c, 0:rows], wf[:, c, :],
                                              start=(c == 0), stop=(c == KD - 1))
                            if n == 2 and next_rows:
                                turn_x(t + 1, next_rows)
                            pe.wait_ge(w_in_sem, 16)
                            if n == 0:
                                pe.wait_ge(qkn_done, t + 1)
                            if n == 2:
                                pe.wait_ge(v_copied, t + 1)
                            for c in range(KD):
                                ins = pe.matmul(out, xnc[:, par, c, 0:rows], wqkv[:, c, n * DA:(n + 1) * DA],
                                                start=(c == 0), stop=(c == KD - 1))
                            ins.then_inc(done, 1)
                        pe.wait_ge(qg_done, t + 1)
                        pe.wait_ge(qkg_done, t + 1)
                        for j in range(2):
                            pe.wait_ge(hT_copied, 4 * t + 2 * j + 2)
                            for a in range(NG):
                                col = (NG * j + a) * P
                                ins = pe.transpose(pH[:, j, a * rows:(a + 1) * rows],
                                                   qk[0:rows, par, col:col + P], ident[0:rows, 0:rows])
                            ins.then_inc(hT_done, 1)
                    pe.sem_inc(v_done, 2)
                    pe.sem_inc(xT_done, 2)
                    pe.sem_inc(hT_done, 4)
                    turn_x(0, P)
                    in_pairs(pe, tile)

        n_project = len(in_use)
        late = attn.enter_context(ExitStack())
        logfT = sb(late, "logfT", [H, T])
        with ExitStack() as ctx:
            PAD = POOL_WINDOWS[-1]
            EXT = HIST + DSEQ
            wu = sb(ctx, "wu", [P, KD, P * (NG - 1)])
            f_rows = sb(ctx, "f_rows", [P, (NT + 1) * H])
            mixw = sb(ctx, "mixw", [P, NG, P])
            pscale = sb(ctx, "pscale", [P, NG])
            bf = sb(ctx, "bf", [H, 1])
            fz = sb(ctx, "fz", [H, T])
            fe = sb(ctx, "fe", [H, T])
            cT = sb(ctx, "cT", [H, SEQ])
            rows_tmp = sb(ctx, "rows_tmp", [P, 2 * DP])
            ones_row = rows_tmp[0:H, 0:SEQ]
            ph, pn = rows_tmp[0:HIST, 0:DP], rows_tmp[0:TS, DP:]
            lf_rows = sb(ctx, "lf_rows", [P, NT + 1, H])
            hist = sb(ctx, "hist", [NSEQ * HIST, DP])
            ue = sb(ctx, "ue", [P, 2, PAD + SEQ])
            us = sb(ctx, "us", [P, 2, NSEQ, EXT])
            un = sb(ctx, "un", [P, 2, TS])
            wa = attnT.rearrange("p g t -> p (g t)")[:, 0:2 * (PAD + SEQ)].rearrange(
                "p (a n) -> p a n", a=2)
            wsm = sb(ctx, "wsm", [P, 2, NSEQ, EXT])
            fix = sb(ctx, "fix", [P, PAD])
            mt = attnT.rearrange("p g t -> p (g t)")[:, 2 * (PAD + SEQ):2 * (PAD + SEQ + T)].rearrange(
                "p (a n) -> p a n", a=2)
            pF = ps(ctx, "pF", [P, 3, 512])
            pM = ps(ctx, "pM", [P, 3, 512])
            pX = pFX[:, 0:NSEQ * HIST]
            pO2 = ps(ctx, "pO2", [P, 512])

            w_in_done, f_in, hist_in = sem("wu_in"), sem("f_in"), sem("hist_in")
            f_raw = sem("f_raw")
            f_mm, f_z, f_abs, f_exp, f_ln, f_min, f_sub = (
                sem("f_mm"), sem("f_z"), sem("f_abs"), sem("f_exp"), sem("f_ln"), sem("f_min"), sem("f_sub"))
            ones_set, scanned, c_scaled, aug_in = sem("ones_set"), sem("scanned"), sem("c_scaled"), sem("aug_in")
            lfT_done, lf_copied, lf_out = sem("lfT_done"), sem("lf_copied"), sem("lf_out")
            pad_set, u_done, u_copied = sem("pad_set"), sem("u_done"), sem("u_copied")
            hx_done, hx_copied = sem("hx_done"), sem("hx_copied")
            pool_step, m_done, mix_done, mix_copied = sem("pool_step"), sem("m_done"), sem("mix_done"), sem("mix_copied")
            pt_done, pt_copied, pool_out = sem("pt_done"), sem("pt_copied"), sem("pool_out")

            finished = [s for s in in_use[:n_project] if all(s is not w for w in (w_q_in, w_k_in, w_v_in))]
            with nc.Block() as block:
                @block.gpsimd
                def _(pool):
                    for s in finished:
                        pool.sem_clear(s)

                @block.sync
                def _(sp):
                    with nc.allow_non_contiguous_dma(reason="a bias and a scale per partition, once"):
                        sp.dma_start(bf[:], b_forget.rearrange("a h -> h a")).then_inc(f_in, 16)
                        sp.dma_start(pscale[:], pool_scale[0].rearrange("(g p) -> p g", p=P)).then_inc(f_in, 16)
                    sp.dma_start(wu[:], win[:, :, P:DP]).then_inc(w_in_done, 16)
                    sp.dma_start(mixw[:], pool_mix_w[0].rearrange("g c d -> c g d")).then_inc(f_in, 16)
                    sp.dma_start(hist[:], state_pool[0].rearrange("b t c -> (b t) c")).then_inc(hist_in, 16)
                    sp.dma_start(pool_sample[0][:, 0:HIST - DSEQ, :], state_pool[0][:, DSEQ:HIST, :]).then_inc(pool_out, 16)
                    sp.wait_ge(c_scaled, 2)
                    sp.dma_start(qT[DH:DH + 1, :, :], fz[:, 0:SEQ]).then_inc(aug_in, 16)
                    sp.dma_start(kT[DH + 1:DH + 2, :, :], fe[:, 0:SEQ]).then_inc(aug_in, 16)
                    sp.wait_ge(lf_copied, 1)
                    sp.dma_start(lfp_out, lf_rows[:, 0:NT, :]).then_inc(lf_out, 16)
                    sp.dma_start(lfs_out, lf_rows[0:TS, NT, :]).then_inc(lf_out, 16)
                    sp.wait_ge(pt_copied, 2 * NG)
                    sp.dma_start(pool_prompt[0, 0], ph).then_inc(pool_out, 16)
                    for b in range(NSEQ):
                        sp.dma_start(pool_sample[0][b, HIST - DSEQ:HIST, :],
                                     pn[b * DSEQ:(b + 1) * DSEQ, :]).then_inc(pool_out, 16)
                    sp.wait_ge(aug_in, 32)
                    sp.wait_ge(lf_out, 32)
                    sp.wait_ge(pool_out, 16 * (2 + NSEQ))

                def mix(pe, g):
                    pe.wait_ge(lf_copied, 1)
                    pe.wait_ge(u_copied, 4 * g + 4)
                    if g:
                        pe.wait_ge(pt_copied, 2 * g)
                    pe.transpose(pO2[0:HIST, 0:P], ue[:, g % 2, PAD + SEQ - HIST:], ident[:])
                    pe.transpose(pO2[0:TS, P:2 * P], un[:, g % 2, :], ident[:]).then_inc(pt_done, 1)
                    pe.wait_ge(m_done, g + 1)
                    if g:
                        pe.wait_ge(mix_copied, 3 * g)
                    for n, (c0, cn) in enumerate(COLS):
                        pe.matmul(pM[:, n, 0:cn], mixw[:, g, :], mt[:, g % 2, c0:c0 + cn],
                                  start=True, stop=True).then_inc(mix_done, 1)

                @block.tensor
                def _(pe):
                    pe.wait_ge(f_raw, 1)
                    for n in range(NT + 1):
                        rows = P if n < NT else TS
                        ins = pe.transpose(pM[0:H, n // 4, n % 4 * P:n % 4 * P + rows], f_rows[0:rows, n * H:(n + 1) * H],
                                           ident[0:rows, 0:rows])
                    ins.then_inc(f_mm, 1)
                    for g in range(NG):
                        if g:
                            pe.wait_ge(u_copied, 4 * g)
                            pe.wait_ge(w_in_done, 16)
                        for n, (c0, cn) in enumerate(COLS):
                            for c in range(KD):
                                lhsT = wu[:, c, (g - 1) * P:g * P] if g else wu0[:, c, :]
                                ins = pe.matmul(pF[:, n, 0:cn], lhsT, xnT[:, c, c0:c0 + cn],
                                                start=(c == 0), stop=(c == KD - 1))
                        ins.then_inc(u_done, 1)
                        pe.wait_ge(hist_in, 16)
                        if g:
                            pe.wait_ge(hx_copied, g)
                        pe.transpose(pX, hist[:, g * P:(g + 1) * P],
                                     ident[0:NSEQ * HIST, 0:NSEQ * HIST]).then_inc(hx_done, 1)
                        if g:
                            mix(pe, g - 1)
                        else:
                            pe.wait_ge(f_sub, 1)
                            for n in range(NT + 1):
                                rows = P if n < NT else TS
                                ins = pe.transpose(pO2[0:rows, n * H:(n + 1) * H], logfT[:, n * P:n * P + rows],
                                                   ident[0:H, 0:H])
                            ins.then_inc(lfT_done, 1)
                    mix(pe, NG - 1)

                def mixed(act, g):
                    for n, (c0, cn) in enumerate(COLS):
                        act.wait_ge(mix_done, 3 * g + n + 1)
                        act.activation(poolT[:, g, c0:c0 + cn], pM[:, n, 0:cn], ACT.Copy,
                                       scale=pscale[:, g:g + 1]).then_inc(mix_copied, 1)

                @block.scalar
                def _(act):
                    act.wait_ge(f_in, 48)
                    act.wait_ge(f_mm, 1)
                    for n, (c0, cn) in enumerate(COLS):
                        ins = act.activation(fz[:, c0:c0 + cn], pM[0:H, n, 0:cn], ACT.Identity, bias=bf[:])
                    ins.then_inc(f_z, 1)
                    act.wait_ge(f_z, 1)
                    act.activation(fe[:], fz[:], ACT.Abs).then_inc(f_abs, 1)
                    act.wait_ge(f_abs, 1)
                    act.activation(fe[:], fe[:], ACT.Exp, scale=-1.0).then_inc(f_exp, 1)
                    act.wait_ge(f_exp, 1)
                    act.activation(fe[:], fe[:], ACT.Ln, bias=1.0).then_inc(f_ln, 1)
                    act.wait_ge(pad_set, 1)
                    for g in range(NG):
                        act.wait_ge(hx_done, g + 1)
                        if g >= 2:
                            act.wait_ge(m_done, g - 1)
                            act.wait_ge(pt_done, g - 1)
                        act.activation(us[:, g % 2, :, 0:HIST],
                                       pX.rearrange("p (b t) -> p b t", t=HIST),
                                       ACT.Copy).then_inc(hx_copied, 1)
                        act.wait_ge(u_done, g + 1)
                        act.activation(ue[:, g % 2, PAD:PAD + SEQ], pF[:, 0:2, :].rearrange("p a b -> p (a b)"),
                                       ACT.Copy).then_inc(u_copied, 2)
                        act.activation(us[:, g % 2, :, HIST:EXT],
                                       pF[:, 2, 0:TS].rearrange("p (b t) -> p b t", t=DSEQ),
                                       ACT.Copy).then_inc(u_copied, 1)
                        act.activation(un[:, g % 2, :], pF[:, 2, 0:TS], ACT.Copy).then_inc(u_copied, 1)
                        if g:
                            mixed(act, g - 1)
                    mixed(act, NG - 1)

                @block.vector
                def _(dve):
                    n_step = [0]

                    def step(ins):
                        n_step[0] += 1
                        ins.then_inc(pool_step, 1)
                        dve.wait_ge(pool_step, n_step[0])

                    dve.tensor_copy(f_rows[:, 0:NT * H], f_logits[:, 0:NT * H])
                    dve.tensor_copy(f_rows[0:TS, NT * H:], f_logits[0:TS, NT * H:]).then_inc(f_raw, 1)
                    dve.memset(ones_row, 1.0).then_inc(ones_set, 1)
                    dve.memset(ue[:, :, 0:PAD], 0.0).then_inc(pad_set, 1)
                    dve.wait_ge(f_z, 1)
                    dve.tensor_scalar(logfT[:], fz[:], 0.0, None, ALU.min).then_inc(f_min, 1)
                    dve.wait_ge(f_min, 1)
                    dve.wait_ge(f_ln, 1)
                    dve.tensor_tensor(logfT[:], logfT[:], fe[:], ALU.subtract).then_inc(f_sub, 1)
                    dve.wait_ge(f_sub, 1)
                    dve.wait_ge(ones_set, 1)
                    dve.tensor_tensor_scan(cT[:], ones_row, logfT[:, 0:SEQ], 0.0, ALU.mult,
                                           ALU.add).then_inc(scanned, 1)
                    dve.wait_ge(scanned, 1)
                    dve.tensor_scalar(fz[:, 0:SEQ], cT[:], INV, None, ALU.mult).then_inc(c_scaled, 1)
                    dve.tensor_scalar(fe[:, 0:SEQ], cT[:], -INV, None, ALU.mult).then_inc(c_scaled, 1)
                    dve.wait_ge(lfT_done, 1)
                    dve.tensor_copy(lf_rows[:, 0:NT, :], pO2[:, 0:NT * H].rearrange("p (n h) -> p n h", h=H))
                    dve.tensor_copy(lf_rows[0:TS, NT, :], pO2[0:TS, NT * H:(NT + 1) * H]).then_inc(lf_copied, 1)
                    for g in range(NG):
                        w = POOL_WINDOWS[g]
                        dve.wait_ge(u_copied, 4 * g + 4)
                        dve.wait_ge(hx_copied, g + 1)
                        src, srcs, first = ue[:, g % 2, :], us[:, g % 2], 0
                        for lvl in range(g + 1):
                            h = 1 << lvl
                            first += h
                            dst, dsts = wa[:, lvl % 2, :], wsm[:, lvl % 2]
                            dve.tensor_tensor(dst[:, first:], src[:, first:], src[:, first - h:PAD + SEQ - h],
                                              ALU.add)
                            step(dve.tensor_tensor(dsts[:, :, first:], srcs[:, :, first:],
                                                   srcs[:, :, first - h:EXT - h], ALU.add))
                            src, srcs = dst, dsts
                        if g >= 2:
                            dve.wait_ge(mix_done, 3 * (g - 1))
                        m = mt[:, g % 2, :]
                        dve.scalar_tensor_tensor(m[:, SEQ:].rearrange("p (b t) -> p b t", t=DSEQ),
                                                 srcs[:, :, HIST:], 1.0 / w, us[:, g % 2, :, HIST:],
                                                 ALU.mult, ALU.subtract)
                        step(dve.scalar_tensor_tensor(m[:, 0:SEQ], src[:, PAD:], 1.0 / w, ue[:, g % 2, PAD:],
                                                      ALU.mult, ALU.subtract))
                        step(dve.tensor_tensor(fix[:, 0:w - 1], src[:, PAD:PAD + w - 1], rcnt[:, 0:w - 1], ALU.mult))
                        dve.tensor_tensor(m[:, 0:w - 1], fix[:, 0:w - 1], ue[:, g % 2, PAD:PAD + w - 1],
                                          ALU.subtract).then_inc(m_done, 1)
                        dve.wait_ge(m_done, g + 1)
                        dve.wait_ge(pt_done, g + 1)
                        dve.tensor_copy(ph[:, g * P:(g + 1) * P], pO2[0:HIST, 0:P]).then_inc(pt_copied, 1)
                        dve.tensor_copy(pn[:, g * P:(g + 1) * P], pO2[0:TS, P:2 * P]).then_inc(pt_copied, 1)

        NB = NT
        GROUPS = [(qb, k0, min(4, qb + 1 - k0)) for qb in range(NB) for k0 in range(0, qb + 1, 4)]
        CHUNKS = [(j, kb, max(512 * j, kb * P)) for j in range(2) for kb in range(4 * (j + 1))]
        NGR, NCH = len(GROUPS), len(CHUNKS)
        HALF_END = [4, NCH]
        MAX_STEP, ROW_STEP = 7, 8
        assert NGR == NCH == 12
        spare += finished
        front.close()
        linv = sb(attn, "linv", [H, SEQ])
        head_rows = sb(attn, "head_rows", [H, H, DH])
        with ExitStack() as ctx:
            qh = sb(ctx, "qh", [DH + 2, SEQ])
            kh = sb(ctx, "kh", [DH + 3, 2, SEQ])
            vh = sb(ctx, "vh", [P, 2, NB, DH + 1])
            expT = sb(ctx, "expT", [P, 3, 512])
            mx_part = sb(ctx, "mx_part", [P, 2, NB])
            mx = sb(ctx, "mx", [P, NB])
            mx_row = sb(ctx, "mx_row", [NB, P])
            pS = ps(ctx, "pS", [P, 2, 512])
            pST = ps(ctx, "pST", [P, 3, 512])
            pOT = ps(ctx, "pOT", [P, 2, 512])
            pMX = ps(ctx, "pMX", [P, 512])

            qh_ready, kh_ready, vh_ready, vh_set = sem("qh_ready"), sem("kh_ready"), sem("vh_ready"), sem("vh_set")
            g_done, part_done, mx_done = sem("g_done"), sem("part_done"), sem("mx_done")
            mxT_done, row_done, row_in = sem("mxT_done"), sem("row_done"), sem("row_in")
            st_done, e_done, pv_done, o_copied = sem("st_done"), sem("e_done"), sem("pv_done"), sem("o_copied")
            l_in, l_set, lb_done, o_scaled = sem("l_in"), sem("l_set"), sem("lb_done"), sem("o_scaled")

            with nc.Block() as block:
                @block.sync
                def _(sp):
                    sp.sem_inc(row_in, 16)
                    with sp.Fori(0, H) as h:
                        sp.wait_ge(row_done, h + 2)
                        sp.dma_start(qT[DH + 2:DH + 3, ds(h, 1), :].rearrange("p a (n t) -> p (a n) t", n=NB),
                                     mx_row[:]).then_inc(row_in, 16)
                    sp.wait_ge(row_in, 16 * (H + 1))
                    sp.wait_ge(o_copied, 4 * H + 4)
                    sp.dma_start(linv[:], qT[DH:DH + 1, :, :]).then_inc(l_in, 16)
                    sp.wait_ge(l_in, 16)

                @block.gpsimd
                def _(pool):
                    pool.memset(vh[:, :, :, DH:], 1.0).then_inc(vh_set, 1)
                    pool.wait_ge(vh_set, 1)
                    with pool.Fori(0, H // 2) as i:
                        for e in range(2):
                            h = 2 * i + e
                            hold(pool, g_done, NGR * h + 12)
                            pool.tensor_copy(qh[:], qT[0:DH + 2, ds(h, 1), :].rearrange("p a t -> p (a t)")
                                             ).then_inc(qh_ready, 1)
                            pool.wait_ge(qh_ready, h + 1)
                            hold(pool, st_done, NCH * h + 12)
                            pool.tensor_copy(kh[:, e, :], kT[:, ds(h, 1), :].rearrange("p a t -> p (a t)")
                                             ).then_inc(kh_ready, 1)
                            pool.wait_ge(kh_ready, h + 1)
                            hold(pool, pv_done, NCH * h + 12)
                            pool.tensor_copy(vh[:, e, :, 0:DH], v_sb[:, 0:NB, ds(h * DH, DH)]).then_inc(vh_ready, 1)
                            pool.wait_ge(vh_ready, h + 1)

                @block.tensor
                def _(pe):
                    def group(h, r):
                        qb, k0, kn = GROUPS[r]
                        if r == 0:
                            pe.wait_ge(qh_ready, h + 1)
                        pe.wait_ge(part_done, NGR * h + r + 1)
                        out = pS[:, r % 2, 0:kn * P]
                        diag = k0 + kn == qb + 1
                        ins = pe.matmul(out, qh[:, qb * P:(qb + 1) * P],
                                        kT[0:DH + 2, ds(h, 1), k0 * P:(k0 + kn) * P].rearrange("p a t -> p (a t)"),
                                        start=True, stop=not diag)
                        if diag:
                            ins = pe.matmul(out[:, (kn - 1) * P:], identb[:], causal[:], start=False, stop=True)
                        ins.then_inc(g_done, 1)

                    def scoresT(h, e, c):
                        j, kb, q0 = CHUNKS[c]
                        n = 512 * (j + 1) - q0
                        if c == 0:
                            pe.wait_ge(kh_ready, h + 1)
                            pe.wait_ge(row_in, 16 * h + 32)
                        pe.wait_ge(e_done, NCH * h + c + 1)
                        diag = q0 == kb * P
                        ins = pe.matmul(pST[:, c % 3, 0:n], kh[:, e, kb * P:(kb + 1) * P],
                                        qT[:, ds(h, 1), q0:q0 + n].rearrange("p a t -> p (a t)"),
                                        start=True, stop=not diag)
                        if diag:
                            ins = pe.matmul(pST[:, c % 3, 0:P], identb[:], causalT[:], start=False, stop=True)
                        ins.then_inc(st_done, 1)

                    def weigh(h, e, c):
                        j, kb, q0 = CHUNKS[c]
                        n = 512 * (j + 1) - q0
                        if c == 0:
                            pe.wait_ge(vh_ready, h + 1)
                        if kb == 0:
                            pe.wait_ge(o_copied, 4 * h + 2 * j + 2)
                        pe.wait_ge(e_done, NCH * h + c + 4)
                        pe.matmul(pOT[0:DH + 1, j, 512 - n:], vh[:, e, kb, :], expT[:, c % 3, 0:n],
                                  start=(kb == 0), stop=(c + 1 in HALF_END)).then_inc(pv_done, 1)

                    def head(h, e, more):
                        for c in range(NCH):
                            scoresT(h, e, c)
                            if more and c < NGR // 2:
                                group(h + 1, 2 * c)
                                group(h + 1, 2 * c + 1)
                            if c:
                                weigh(h, e, c - 1)
                            if more and c == ROW_STEP:
                                turn_maxima(h + 1)
                        weigh(h, e, NCH - 1)

                    def turn_maxima(h):
                        pe.wait_ge(mx_done, h + 2)
                        pe.wait_ge(row_done, h + 1)
                        pe.transpose(pMX[0:NB, 0:P], mx[:], ident[:]).then_inc(mxT_done, 1)
                    pe.sem_inc(g_done, 12)
                    pe.sem_inc(st_done, 24)
                    pe.sem_inc(pv_done, 24)
                    pe.sem_inc(mxT_done, 1)
                    for r in range(NGR):
                        group(0, r)
                    turn_maxima(0)
                    with pe.Fori(0, H // 2 - 1) as i:
                        for e in range(2):
                            head(2 * i + e, e, True)
                    head(H - 2, 0, True)
                    head(H - 1, 1, False)

                @block.scalar
                def _(act):
                    def exps(h, c):
                        j, kb, q0 = CHUNKS[c]
                        n = 512 * (j + 1) - q0
                        act.wait_ge(st_done, NCH * h + c + 25)
                        act.wait_ge(pv_done, NCH * h + c + 22)
                        act.activation(expT[:, c % 3, 0:n], pST[:, c % 3, 0:n], ACT.Exp, scale=SCALE
                                       ).then_inc(e_done, 1)
                    act.sem_inc(e_done, 3)
                    with act.Fori(0, H) as h:
                        for c in range(NCH):
                            exps(h, c)

                @block.vector
                def _(dve):
                    def maxima(h, r):
                        qb, k0, kn = GROUPS[r]
                        if r == 0:
                            dve.wait_ge(mx_done, h + 1)
                        dve.wait_ge(g_done, NGR * h + r + 13)
                        dve.tensor_reduce(mx_part[:, k0 // 4, qb:qb + 1], pS[:, r % 2, 0:kn * P], AX.X,
                                          ALU.max).then_inc(part_done, 1)

                    def combine(h):
                        dve.wait_ge(part_done, NGR * h + NGR + 2)
                        dve.wait_ge(mxT_done, h + 1)
                        dve.tensor_tensor(mx[:], mx_part[:, 0], mx_part[:, 1], ALU.max).then_inc(mx_done, 1)

                    def rows(h):
                        dve.wait_ge(mxT_done, h + 2)
                        dve.wait_ge(row_in, 16 * h + 16)
                        dve.tensor_scalar(mx_row[:], pMX[0:NB, 0:P], -1.0, None, ALU.mult).then_inc(row_done, 1)

                    def outputs(h, i, e, j):
                        cols = slice(512 * j, 512 * (j + 1))
                        dve.wait_ge(pv_done, NCH * h + HALF_END[j] + 24)
                        dve.tensor_copy(attnT[e * DH:(e + 1) * DH, ds(i, 1), cols].rearrange("p a t -> p (a t)"),
                                        pOT[0:DH, j, :]).then_inc(o_copied, 1)
                        dve.tensor_copy(qT[DH:DH + 1, ds(h, 1), cols].rearrange("p a t -> p (a t)"),
                                        pOT[DH:DH + 1, j, :]).then_inc(o_copied, 1)

                    def head(h, i, e, more):
                        for c in range(NCH):
                            if more and c < NGR // 2:
                                maxima(h + 1, 2 * c)
                                maxima(h + 1, 2 * c + 1)
                            if more and c == MAX_STEP:
                                combine(h + 1)
                            if more and c == ROW_STEP:
                                rows(h + 1)
                            if c == HALF_END[0]:
                                outputs(h, i, e, 0)
                        outputs(h, i, e, 1)
                    dve.sem_inc(part_done, 2)
                    dve.sem_inc(row_done, 1)
                    dve.sem_inc(o_copied, 4)
                    dve.memset(mx_part[:, 1, :], LOWEST).then_inc(mx_done, 1)
                    dve.wait_ge(mx_done, 1)
                    for r in range(NGR):
                        maxima(0, r)
                    combine(0)
                    rows(0)
                    with dve.Fori(0, H // 2 - 1) as i:
                        for e in range(2):
                            head(2 * i + e, i, e, True)
                    head(H - 2, H // 2 - 1, 0, True)
                    head(H - 1, H // 2 - 1, 1, False)

        w0 = v_sb[:].rearrange("p a b -> p (a b)")
        wg1 = sb(attn, "wg1", [P, 2, KD, P])
        wg = [w0[:, 0:2 * D].rearrange("p (j c n) -> p j c n", j=2, c=KD), wg1]
        wbr = [w0[:, (2 + par) * D:(3 + par) * D].rearrange("p (j c n) -> p j c n", j=2, c=NG)
               for par in range(2)]
        wm_in = [sem("wm_in0"), sem("wm_in1")]

        def load_columns(sp, n, par):
            for j, col in enumerate((GA0, GB0)):
                sp.dma_start(wg[par][:, j], win[:, :, ds(n * P + col, P)]).then_inc(wm_in[par], 16)
            for j, w in enumerate((w_branch_pool, w_branch_attn)):
                sp.dma_start(wbr[par][:, j], w[0].rearrange("(c p) n -> p c n", p=P)[:, :, ds(n * P, P)]
                             ).then_inc(wm_in[par], 16)
        with ExitStack() as ctx:
            kp, vp = (heads[:, j * 2 * PAST * NG:(j + 1) * 2 * PAST * NG].rearrange(
                "p (a n c) -> p a n c", a=2, n=NPAGES) for j in range(2))
            kpT = heads[:, 4 * PAST * NG:6 * PAST * NG].rearrange("p (a g k) -> p a g k", a=2, g=NG)
            lfp = sb(ctx, "lfp", [P, 2, NPAGES, H])
            vn = sb(ctx, "vn", [DSEQ, 2, DA])
            lfr = sb(ctx, "lfr", [H, ALLK])
            cr = sb(ctx, "cr", [H, ALLK])
            ones = sb(ctx, "ones", [H, ALLK])
            cq = sb(ctx, "cq", [H, DSEQ])
            C_ROW = 32
            aug_q = sb(ctx, "aug_q", [C_ROW + H, TS])
            aug_k = sb(ctx, "aug_k", [C_ROW + H, ALLK])
            qbd = sb(ctx, "qbd", [P, NG * (H * DSEQ + 2 * DSEQ)])
            pr = sb(ctx, "pr", [TS, ALLK])
            prn = sb(ctx, "prn", [P, ALLK])
            prT = sb(ctx, "prT", [P, (NPAGES + 1) * TS])
            dmx = [sb(ctx, f"dmx{i}", [TS, 1]) for i in range(4)]
            pC = ps(ctx, "pC", [P, 512])
            pK = ps(ctx, "pK", [P, 2, 512])
            pSS = ps(ctx, "pSS", [P, 1024])
            pP = ps(ctx, "pP", [P, 512])
            pOO = ps(ctx, "pOO", [P, 512])

            k_in = [sem("k_in0"), sem("k_in1")]
            vc_in = [sem("vc_in0"), sem("vc_in1")]
            lf_in = [sem("lf_in0"), sem("lf_in1")]
            d_cleared = sem("d_cleared")
            d_set, lT_done, lT_copied, lr_new = sem("d_set"), sem("lT_done"), sem("lT_copied"), sem("lr_new")
            d_scan, d_ncr, d_cq, d_rows, qbd_done = sem("d_scan"), sem("d_ncr"), sem("d_cq"), sem("d_rows"), sem("qbd_done")
            kT_done, kT_copied = sem("kT_done"), [sem("kT_copied0"), sem("kT_copied1")]
            ds_done, dmx_done, dnm_done, de_done = sem("ds_done"), sem("dmx_done"), sem("dnm_done"), sem("de_done")
            dr_done, dn_done, dT_done, dT_copied = sem("dr_done"), sem("dn_done"), sem("dT_done"), sem("dT_copied")
            do_done, do_copied = sem("do_done"), sem("do_copied")

            with nc.Block() as block:
                @block.sync
                def _(sp):
                    load_columns(sp, 0, 0)
                    with sp.Fori(0, NSEQ // 2) as i:
                        for par in range(2):
                            b = 2 * i + par
                            pg = [sp.value_load(pages[0:1, ds(b * NPAGES + j, 1)], min_val=0, max_val=NPHYS - 1)
                                  for j in range(NPAGES)]
                            sp.wait_ge(lT_done, b + 1)
                            for j in range(NPAGES):
                                sp.dma_start(lfp[:, par, j, :], clf[ds(pg[j], 1)].rearrange("a t h -> (a t) h")
                                             ).then_inc(lf_in[par], 16)
                            sp.wait_ge(kT_done, 4 * b + 4)
                            for j in range(NPAGES):
                                sp.dma_start(kp[:, par, j, :], ck[ds(pg[j], 1)].rearrange("a t n -> (a t) n")
                                             ).then_inc(k_in[par], 16)
                            sp.wait_ge(do_done, b + 1)
                            for j in range(NPAGES):
                                sp.dma_start(vp[:, par, j, :], cv[ds(pg[j], 1)].rearrange("a t n -> (a t) n")
                                             ).then_inc(vc_in[par], 16)
                            sp.dma_start(vn[:, par, :], vs_out[ds(b * DSEQ, DSEQ), :]).then_inc(vc_in[par], 16)

                @block.tensor
                def _(pe):
                    def turn_pages(b, i, par):
                        pe.wait_ge(lf_in[par], 16 * NPAGES * (i + 1))
                        pe.wait_ge(lT_copied, b + 1)
                        for j in range(NPAGES):
                            ins = pe.transpose(pC[0:H, j * P:(j + 1) * P], lfp[:, par, j, :], ident[:])
                        ins.then_inc(lT_done, 1)
                        pe.wait_ge(k_in[par], 16 * NPAGES * (i + 1))
                        for p in range(NG):
                            pe.wait_ge(kT_copied[p % 2], 2 * b + p // 2 + 1)
                            for j in range(NPAGES):
                                ins = pe.transpose(pK[:, p % 2, j * P:(j + 1) * P],
                                                   kp[:, par, j, p * P:(p + 1) * P], ident[:])
                            ins.then_inc(kT_done, 1)

                    def scores(b, par):
                        pe.wait_ge(qbd_done, b + 1)
                        pe.wait_ge(d_rows, b + 1)
                        pe.wait_ge(de_done, b + 1)
                        for part in range(2):
                            cols = slice(0, PAST) if part == 0 else slice(PAST, ALLK)
                            out = pSS[0:TS, cols]
                            for p in range(NG):
                                if part == 0:
                                    pe.wait_ge(kT_copied[p % 2], 2 * b + p // 2 + 2)
                                rhs = kpT[:, par, p, :] if part == 0 else kT2[:, p, ds(b * DSEQ, DSEQ)]
                                pe.matmul(out, qbd[:, p * TS:(p + 1) * TS], rhs, start=(p == 0), stop=False)
                            pe.matmul(out, aug_q[:], aug_k[:, cols], start=False, stop=(part == 0))
                        pe.matmul(out, rep_q[:].rearrange("p h q -> p (h q)"), causal8[:], start=False,
                                  stop=True).then_inc(ds_done, 1)

                    def outputs(b, i, par):
                        pe.wait_ge(dn_done, b + 1)
                        pe.wait_ge(dT_copied, b + 1)
                        for j in range(NPAGES):
                            pe.matmul(pP[:, j * TS:(j + 1) * TS], prn[:, j * P:(j + 1) * P], ident[:, 0:TS],
                                      start=True, stop=True)
                        pe.matmul(pP[0:DSEQ, NPAGES * TS:(NPAGES + 1) * TS], prn[:, PAST:ALLK],
                                  ident[:, 0:TS], start=True, stop=True).then_inc(dT_done, 1)
                        pe.wait_ge(vc_in[par], 16 * (NPAGES + 1) * (i + 1))
                        pe.wait_ge(dT_copied, b + 2)
                        pe.wait_ge(do_copied, b + 1)
                        for p in range(NG):
                            out, qs = pOO[:, p * 2 * DSEQ:(p + 1) * 2 * DSEQ], p * 2 * DSEQ
                            for j in range(NPAGES):
                                pe.matmul(out, vp[:, par, j, p * P:(p + 1) * P],
                                          prT[:, j * TS + qs:j * TS + qs + 2 * DSEQ], start=(j == 0), stop=False)
                            ins = pe.matmul(out, vn[:, par, p * P:(p + 1) * P],
                                            prT[0:DSEQ, NPAGES * TS + qs:NPAGES * TS + qs + 2 * DSEQ],
                                            start=False, stop=True)
                        ins.then_inc(do_done, 1)

                    def pair(i, last):
                        b = 2 * i
                        scores(b, 0)
                        turn_pages(b + 1, i, 1)
                        outputs(b, i, 0)
                        scores(b + 1, 1)
                        if not last:
                            turn_pages(b + 2, i + 1, 0)
                        outputs(b + 1, i, 1)
                    pe.sem_inc(kT_done, 8)
                    pe.sem_inc(do_done, 2)
                    pe.sem_inc(lT_done, 2)
                    pe.wait_ge(d_set, 5)
                    pe.sem_inc(ds_done, 2)
                    pe.sem_inc(dT_done, 1)
                    for n in range(2 * NG):
                        j, g = divmod(n, NG)
                        pe.wait_ge(l_set, j + 2)
                        if n >= 2:
                            pe.wait_ge(o_scaled, n - 1)
                        pe.matmul(pK[:, n % 2, :], head_rows[:, 2 * g:2 * g + 2, :].rearrange("p h d -> p (h d)"),
                                  linv[:, j * 512:(j + 1) * 512], start=True, stop=True).then_inc(lb_done, 1)
                    pe.wait_ge(o_scaled, 2 * NG)
                    turn_pages(0, 0, 0)
                    with pe.Fori(0, NSEQ // 2 - 1) as i:
                        pair(i, False)
                    pair(NSEQ // 2 - 1, True)

                @block.scalar
                def _(act):
                    def copy_keys(b, par):
                        for p in (1, 3):
                            act.wait_ge(kT_done, 4 * b + p + 9)
                            act.wait_ge(ds_done, b + 1)
                            act.activation(kpT[:, par, p, :], pK[:, 1, :], ACT.Copy).then_inc(kT_copied[1], 1)

                    def exps(b):
                        act.wait_ge(dnm_done, b + 1)
                        act.activation(pr[:], pSS[0:TS, 0:ALLK], ACT.Exp, bias=dmx[1][:], scale=SCALE,
                                       accum_out=dmx[2][:]).then_inc(de_done, 1)

                    def pair(i, last):
                        b = 2 * i
                        exps(b)
                        copy_keys(b + 1, 1)
                        exps(b + 1)
                        if not last:
                            copy_keys(b + 2, 0)
                    act.sem_inc(kT_copied[1], 1)
                    act.sem_inc(de_done, 1)
                    copy_keys(0, 0)
                    with act.Fori(0, NSEQ // 2 - 1) as i:
                        pair(i, False)
                    pair(NSEQ // 2 - 1, True)

                @block.vector
                def _(dve):
                    qcols = qbd[:].rearrange("p (g s) -> p g s", s=TS + 2 * DSEQ)

                    def gates(b):
                        dve.wait_ge(lT_done, b + 3)
                        dve.tensor_copy(lfr[:, 0:PAST], pC[0:H, :]).then_inc(lT_copied, 1)
                        dve.tensor_copy(lfr[:, PAST:ALLK], logfT[:, ds(SEQ + b * DSEQ, DSEQ)]).then_inc(lr_new, 1)
                        dve.wait_ge(lT_copied, b + 2)
                        dve.wait_ge(lr_new, b + 1)
                        dve.tensor_tensor_scan(cr[:], ones[:], lfr[:], 0.0, ALU.mult, ALU.add).then_inc(d_scan, 1)
                        dve.wait_ge(d_scan, b + 1)
                        dve.wait_ge(ds_done, b + 2)
                        dve.tensor_scalar(aug_k[0:H, :], cr[:], -INV, None, ALU.mult).then_inc(d_ncr, 1)
                        dve.tensor_scalar(cq[:], cr[:, PAST:ALLK], INV, None, ALU.mult).then_inc(d_cq, 1)
                        for e in range(2):
                            ins = dve.tensor_copy(qcols[e * DH:(e + 1) * DH, :, e * DSEQ:(e + 1) * DSEQ],
                                                  qT2[e * DH:(e + 1) * DH, :, ds(b * DSEQ, DSEQ)])
                        ins.then_inc(qbd_done, 1)
                        dve.wait_ge(d_cq, b + 1)
                        dve.wait_ge(d_ncr, b + 1)
                        dve.tensor_tensor(aug_q[C_ROW:C_ROW + H, :].rearrange("p (h q) -> p h q", h=H), same_head[:],
                                          cq[:].unsqueeze(1).to_broadcast([H, H, DSEQ]), ALU.mult).then_inc(d_rows, 1)

                    def copy_keys(b, par, p):
                        dve.wait_ge(kT_done, 4 * b + p + 9)
                        dve.wait_ge(ds_done, b + 1)
                        dve.tensor_copy(kpT[:, par, p, :], pK[:, 0, :]).then_inc(kT_copied[0], 1)

                    def sequence(b, par, more):
                        dve.wait_ge(ds_done, b + 3)
                        dve.tensor_reduce(dmx[0][:], pSS[0:TS, 0:ALLK], AX.X, ALU.max).then_inc(dmx_done, 1)
                        dve.wait_ge(dmx_done, b + 1)
                        dve.tensor_scalar(dmx[1][:], dmx[0][:], -SCALE, None, ALU.mult).then_inc(dnm_done, 1)
                        if more:
                            copy_keys(b + 1, 1 - par, 0)
                        dve.wait_ge(de_done, b + 2)
                        dve.reciprocal(dmx[3][:], dmx[2][:]).then_inc(dr_done, 1)
                        dve.wait_ge(dr_done, b + 1)
                        dve.wait_ge(dT_done, b + 1)
                        dve.tensor_scalar(prn[0:TS, :], pr[:], dmx[3][:], None, ALU.mult).then_inc(dn_done, 1)
                        if more:
                            copy_keys(b + 1, 1 - par, 2)
                        dve.wait_ge(dT_done, b + 2)
                        dve.wait_ge(do_copied, b + 1)
                        dve.tensor_copy(prT[:, 0:NPAGES * TS], pP[:, 0:NPAGES * TS])
                        dve.tensor_copy(prT[0:DSEQ, NPAGES * TS:], pP[0:DSEQ, NPAGES * TS:(NPAGES + 1) * TS]
                                        ).then_inc(dT_copied, 1)
                        if more:
                            gates(b + 1)
                        dve.wait_ge(do_done, b + 3)
                        pairs = pOO[:, 0:TS].rearrange("d (g e q) -> d g e q", e=2, q=DSEQ)
                        for e in range(2):
                            rows = slice(e * DH, (e + 1) * DH)
                            ins = dve.tensor_copy(attnT[rows, :, ds(SEQ + b * DSEQ, DSEQ)], pairs[rows, :, e, :])
                        ins.then_inc(do_copied, 1)

                    def pair(i, last):
                        sequence(2 * i, 0, True)
                        sequence(2 * i + 1, 1, not last)
                    dve.memset(ones[:], 1.0).then_inc(d_set, 1)
                    dve.memset(qbd[:], 0.0).then_inc(d_set, 1)
                    dve.memset(prn[:], 0.0).then_inc(d_set, 1)
                    dve.memset(aug_q[:], 0.0).then_inc(d_cleared, 1)
                    dve.memset(aug_k[:], 0.0).then_inc(d_cleared, 1)
                    dve.wait_ge(d_cleared, 2)
                    dve.tensor_copy(aug_q[0:H, :], same_head[:].rearrange("p h q -> p (h q)")).then_inc(d_set, 1)
                    dve.memset(aug_k[C_ROW:C_ROW + H, :], 1.0).then_inc(d_set, 1)
                    dve.wait_ge(d_set, 5)
                    dve.sem_inc(lT_copied, 1)
                    dve.sem_inc(kT_copied[0], 1)
                    dve.sem_inc(dT_copied, 1)
                    dve.sem_inc(do_copied, 1)
                    dve.tensor_copy(head_rows[:], same_head[:, :, 0:1].to_broadcast([H, H, DH])).then_inc(l_set, 1)
                    for j in range(2):
                        half = linv[:, j * 512:(j + 1) * 512]
                        dve.reciprocal(half, half).then_inc(l_set, 1)
                    for n in range(2 * NG):
                        j, g = divmod(n, NG)
                        dve.wait_ge(lb_done, n + 1)
                        half = attnT[:, g, j * 512:(j + 1) * 512]
                        dve.tensor_tensor(half, half, pK[:, n % 2, :], ALU.mult).then_inc(o_scaled, 1)
                    gates(0)
                    copy_keys(0, 0, 0)
                    copy_keys(0, 0, 2)
                    with dve.Fori(0, NSEQ // 2 - 1) as i:
                        pair(i, False)
                    pair(NSEQ // 2 - 1, True)

        mixedT = work[:, 0:KD * T].rearrange("p (c t) -> p c t", c=KD)
        wout = work[:, KD * T:KD * (T + D)].rearrange("p (c n) -> p c n", c=KD)
        with ExitStack() as ctx:
            with ExitStack() as inner:
                sg = sb(inner, "sg", [P, 2, 2, 512])
                pG = ps(inner, "pG", [P, 2, 4, 512])

                NC3 = len(COLS)
                wout_in = sem("wout_in")
                g_done, br_done, sg_done = sem("g_done"), sem("br_done"), sem("sg_done")
                prod_a, prod_b, merged = sem("prod_a"), sem("prod_b"), sem("merged")

                with nc.Block() as block:
                    @block.sync
                    def _(sp):
                        load_columns(sp, 1, 1)
                        with sp.Fori(1, KD // 2) as i:
                            for par in range(2):
                                n = 2 * i + par
                                sp.wait_ge(br_done, NC3 * n + NC3 - 2 + 2)
                                load_columns(sp, n, par)

                    @block.gpsimd
                    def _(pool):
                        pool.dma_start(wout[:], w_out[0].rearrange("(c p) n -> p c n", p=P)).then_inc(wout_in, 16)
                        pool.wait_ge(wout_in, 16)

                    @block.tensor
                    def _(pe):
                        pe.sem_inc(br_done, 6)
                        with pe.Fori(0, KD // 2) as i:
                            for par in range(2):
                                pe.wait_ge(wm_in[par], 64 * i + 64)
                                for c, (c0, cn) in enumerate(COLS):
                                    m = NC3 * (2 * i + par) + c
                                    mp = (NC3 * par + c) % 2
                                    pe.wait_ge(merged, m + 1)
                                    for j in range(2):
                                        for d in range(KD):
                                            ins = pe.matmul(pG[:, mp, j, 0:cn], wg[par][:, j, d, :], xnT[:, d, c0:c0 + cn],
                                                            start=(d == 0), stop=(d == KD - 1))
                                        ins.then_inc(g_done, 1)
                                    for j, br in enumerate((poolT, attnT)):
                                        for d in range(NG):
                                            ins = pe.matmul(pG[:, mp, 2 + j, 0:cn], wbr[par][:, j, d, :], br[:, d, c0:c0 + cn],
                                                            start=(d == 0), stop=(d == NG - 1))
                                    ins.then_inc(br_done, 1)

                    @block.scalar
                    def _(act):
                        with act.Fori(0, KD // 2) as i:
                            for mm in range(2 * NC3):
                                m = 2 * NC3 * i + mm
                                cn = COLS[mm % NC3][1]
                                act.wait_ge(merged, m + 1)
                                for j in range(2):
                                    act.wait_ge(g_done, 2 * m + j + 1)
                                    act.activation(sg[:, mm % 2, j, 0:cn], pG[:, mm % 2, j, 0:cn],
                                                   ACT.Sigmoid).then_inc(sg_done, 1)

                    @block.vector
                    def _(dve):
                        dve.sem_inc(merged, 2)
                        with dve.Fori(0, KD // 2) as i:
                            for mm in range(2 * NC3):
                                m = 2 * NC3 * i + mm
                                c0, cn = COLS[mm % NC3]
                                a, b = sg[:, mm % 2, 0, 0:cn], sg[:, mm % 2, 1, 0:cn]
                                dve.wait_ge(br_done, m + 7)
                                dve.wait_ge(sg_done, 2 * m + 2)
                                dve.tensor_tensor(a, a, pG[:, mm % 2, 2, 0:cn], ALU.mult).then_inc(prod_a, 1)
                                dve.tensor_tensor(b, b, pG[:, mm % 2, 3, 0:cn], ALU.mult).then_inc(prod_b, 1)
                                dve.wait_ge(prod_a, m + 1)
                                dve.wait_ge(prod_b, m + 1)
                                dst = mixedT[:, ds(2 * i + mm // NC3, 1), c0:c0 + cn].rearrange("p a t -> p (a t)")
                                dve.tensor_tensor(dst, a, b, ALU.add).then_inc(merged, 1)

        attn.close()

        NGP = NPICK // RING
        BOTH = NPC // PH
        HEAD_STEPS, LAST_STEPS = 8, 18
        AHEAD = 2 * RING
        CR = AHEAD + 1
        HALF = NPICK // 2
        CHAIN = PH * HEAD_STEPS + LAST_STEPS
        PIECES = {2: (0, 1), 3: (2,), 4: (3, 4), 5: (5,), 6: (6, 7), 7: (8,), 8: (9,), 9: (10, 11), 10: (12,),
                  11: (13,), 12: (14, 15)}
        assert NGP == 16 and PH == 8 and NPICK % RING == 0
        with ExitStack() as ctx:
            wq = inputs[:, 0:KD * NPC * P].rearrange("p (c n) -> p c n", c=KD)
            subT = sb(ctx, "subT", [P, NPC, NK])
            hn_next = sb(ctx, "hn_next", [P, D])
            hnT = sb(ctx, "hnT", [P, KD, P])
            qTp = sb(ctx, "qTp", [P, 2, BOTH, P])
            s_sb = sb(ctx, "s_sb", [P, 2, BOTH, NK])
            s_rest = sb(ctx, "s_rest", [P, BOTH, NK])
            v16 = sb(ctx, "v16", [P, NPC, TOPK])
            i16 = sb(ctx, "i16", [P, NPC, TOPK], U32)
            i16f = sb(ctx, "i16f", [P, NPC, TOPK])
            cand = sb(ctx, "cand", [P, TOPK * TOPK])
            cand_rest = sb(ctx, "cand_rest", [P, TOPK * TOPK])
            top_s = sb(ctx, "top_s", [P, PH, TOPK])
            top_p = sb(ctx, "top_p", [P, PH, TOPK], U32)
            part_i = sb(ctx, "part_i", [P, 2, PH, TOPK], U32)
            part_f = sb(ctx, "part_f", [P, 2, PH, TOPK])
            iota16 = sb(ctx, "iota16", [P, TOPK])
            eq = sb(ctx, "eq", [P, PH // 2, TOPK, TOPK])
            half_i = sb(ctx, "half_i", [P, 2, PH, TOPK])
            idx_f = sb(ctx, "idx_f", [P, NPICK])
            idx_next = sb(ctx, "idx_next", [P, NPICK], U32)
            dif = sb(ctx, "dif", [P, PH, TOPK])
            gsum = sb(ctx, "gsum", [P, PH])
            ginv = sb(ctx, "ginv", [P, PH])
            gw_next = sb(ctx, "gw_next", [P, NPICK])
            pA = ps(ctx, "pA", [P, 2, 512])
            pB = ps(ctx, "pB", [P, 2, 512])
            sk = [inputs[:, KD * NPC * P:], eq[:].rearrange("p h a b -> p (h a b)")]

            wq_in = [sem(f"wq_in{c}") for c in range(4)]
            sk_in, skT_done, skT_copied, it_set = sem("sk_in"), sem("skT_done"), sem("skT_copied"), sem("it_set")
            hn_in, hn_moved, hnT_done, hnT_copied = sem("hn_in"), sem("hn_moved"), sem("hnT_done"), sem("hnT_copied")
            qT_done, qT_copied, sc_done, sc_copied, sc_used = (
                sem("qT_done"), sem("qT_copied"), sem("sc_done"), sem("sc_copied"), sem("sc_used"))
            top_step, dif_done, gexp_done, idx_ready, idx_moved = (
                sem("top_step"), sem("dif_done"), sem("gexp_done"), sem("idx_ready"), sem("idx_moved"))
            gw_moved = sem("gw_moved")

            def pe_choose(pe, f, g, rows, first=False):
                if g == 0:
                    pe.wait_ge(sc_copied, 8 * f + 2)
                    for j in range(2):
                        for a in range(4):
                            c = 4 * j + a
                            ins = pe.transpose(pA[:, j, a * P:a * P + rows], hn_next[0:rows, c * P:(c + 1) * P],
                                               ident[0:rows, 0:rows])
                        ins.then_inc(hnT_done, 1)
                if 2 <= g < 2 + PH:
                    e = g - 2
                    pe.wait_ge(hnT_copied, 2 * f + 2)
                    pe.wait_ge(qT_copied, 8 * f + e + 1)
                    if first and e % 2 == 0:
                        pe.wait_ge(wq_in[e // 2], 16)
                    for c in range(BOTH):
                        for d in range(KD):
                            col = (BOTH * e + c) * P
                            ins = pe.matmul(pB[:, e % 2, c * P:c * P + rows], wq[:, d, col:col + P],
                                            hnT[:, d, 0:rows], start=(d == 0), stop=(d == KD - 1))
                    ins.then_inc(qT_done, 1)
                if 3 <= g < 3 + PH:
                    e = g - 3
                    pe.wait_ge(qT_copied, 8 * f + e + 3)
                    pe.wait_ge(sc_copied, 8 * f + e + 1)
                    for c in range(BOTH):
                        ins = pe.matmul(pA[0:rows, e % 2, c * NK:(c + 1) * NK], qTp[:, e % 2, c, 0:rows],
                                        subT[:, BOTH * e + c, :], start=True, stop=True)
                    ins.then_inc(sc_done, 1)

            def act_choose(act, f, g, rows):
                if g == 0:
                    for j in range(2):
                        act.wait_ge(hnT_done, 2 * f + j + 1)
                        act.activation(hnT[:, 4 * j:4 * j + 4, 0:rows],
                                       pA[:, j, :].rearrange("p (a b) -> p a b", a=4)[:, :, 0:rows],
                                       ACT.Copy).then_inc(hnT_copied, 1)
                if 2 <= g < 2 + PH:
                    e = g - 2
                    act.wait_ge(qT_done, 8 * f + e + 1)
                    act.wait_ge(sc_done, 8 * f + e + 1)
                    act.activation(qTp[:, e % 2, :, 0:rows],
                                   pB[:, e % 2, 0:BOTH * P].rearrange("p (a b) -> p a b", a=BOTH)[:, :, 0:rows],
                                   ACT.Copy).then_inc(qT_copied, 1)
                if 3 <= g < 3 + PH:
                    e = g - 3
                    act.wait_ge(sc_done, 8 * f + e + 3)
                    act.wait_ge(sc_used, 8 * f + e + 1)
                    act.activation(s_sb[0:rows, e % 2].rearrange("p a b -> p (a b)"),
                                   pA[0:rows, e % 2, 0:BOTH * NK], ACT.Copy).then_inc(sc_copied, 1)
                if g == 13:
                    act.wait_ge(dif_done, f + 1)
                    act.activation(dif[0:rows], dif[0:rows], ACT.Exp).then_inc(gexp_done, 1)

            def dve_choose(dve, f, g, rows, count, first=False):
                def step(ins):
                    count[0] += 1
                    ins.then_inc(top_step, 1)
                    hold(dve, top_step, CHAIN * f + count[0])

                R = slice(0, rows)
                packed = [(0, slice(0, NPICK))] if rows == P else [(0, slice(0, HALF)), (TS, slice(HALF, NPICK))]
                if 4 <= g < 4 + PH:
                    e = g - 4
                    hold(dve, sc_copied, 8 * f + e + 3)
                    sides = [(c, s_sb[R, e % 2, c, :], s_rest[R, c, :], BOTH * e + c) for c in range(BOTH)]
                    for c, s, rest, n in sides:
                        ins = dve.max(v16[R, n, 0:8], s)
                    step(ins)
                    for c, s, rest, n in sides:
                        dve.max_index(i16[R, n, 0:8], v16[R, n, 0:8], s)
                        ins = dve.match_replace(rest, v16[R, n, 0:8], s, LOWEST)
                    step(ins)
                    for c, s, rest, n in sides:
                        ins = dve.max(v16[R, n, 8:16], rest)
                    step(ins)
                    for c, s, rest, n in sides:
                        ins = dve.max_index(i16[R, n, 8:16], v16[R, n, 8:16], rest)
                    ins.then_inc(sc_used, 1)
                    step(dve.tensor_tensor(cand[R, :].rearrange("p (a b) -> p a b", a=TOPK),
                                           v16[R, 2 * e, :].unsqueeze(2).to_broadcast([rows, TOPK, TOPK]),
                                           v16[R, 2 * e + 1, :].unsqueeze(1).to_broadcast([rows, TOPK, TOPK]), ALU.add))
                    step(dve.max(top_s[R, e, 0:8], cand[R, :]))
                    dve.max_index(top_p[R, e, 0:8], top_s[R, e, 0:8], cand[R, :])
                    step(dve.match_replace(cand_rest[R, :], top_s[R, e, 0:8], cand[R, :], LOWEST))
                    step(dve.max(top_s[R, e, 8:16], cand_rest[R, :]))
                    step(dve.max_index(top_p[R, e, 8:16], top_s[R, e, 8:16], cand_rest[R, :]))
                if g == 12:
                    dve.tensor_tensor(dif[R], top_s[R], top_s[R, :, 0:1].to_broadcast([rows, PH, TOPK]),
                                      ALU.subtract).then_inc(dif_done, 1)
                    dve.tensor_scalar(part_i[R, 0], top_p[R], 4, None, ALU.logical_shift_right)
                    dve.tensor_copy(i16f[R], i16[R])
                    step(dve.tensor_scalar(part_i[R, 1], top_p[R], TOPK - 1, None, ALU.bitwise_and))
                    step(dve.tensor_copy(part_f[R], part_i[R]))
                if g >= 12:
                    side, half = divmod(g - 12, 2)
                    hs_ = slice(half * PH // 2, (half + 1) * PH // 2)
                    numbers = i16f[R].rearrange("p (h c) k -> p c h k", c=2)[:, side, hs_, :]
                    shape = [rows, PH // 2, TOPK, TOPK]
                    step(dve.tensor_tensor(eq[R], part_f[R, side, hs_, :].unsqueeze(3).to_broadcast(shape),
                                           iota16[R].unsqueeze(1).unsqueeze(1).to_broadcast(shape), ALU.is_equal))
                    step(dve.tensor_tensor(eq[R], eq[R], numbers.unsqueeze(2).to_broadcast(shape), ALU.mult))
                    step(dve.tensor_reduce(half_i[R, side, hs_, :], eq[R], AX.X, ALU.add))
                if g == 14:
                    dve.wait_ge(gexp_done, f + 1)
                    step(dve.tensor_reduce(gsum[R], dif[R], AX.X, ALU.add))
                    step(dve.reciprocal(ginv[R], gsum[R]))
                    if not first:
                        dve.wait_ge(gw_moved, f)
                    for r0, picks in packed:
                        hh = slice(picks.start // TOPK, picks.stop // TOPK)
                        ins = dve.tensor_tensor(
                            gw_next[r0:r0 + rows, 0:picks.stop - picks.start].rearrange("p (h k) -> p h k", k=TOPK),
                            dif[R, hh], ginv[R, hh].unsqueeze(2).to_broadcast([rows, hh.stop - hh.start, TOPK]), ALU.mult)
                    step(ins)
                if g == 15:
                    step(dve.scalar_tensor_tensor(idx_f[R], half_i[R, 0].rearrange("p h k -> p (h k)"), float(NK),
                                                  half_i[R, 1].rearrange("p h k -> p (h k)"), ALU.mult, ALU.add))
                    if not first:
                        dve.wait_ge(idx_moved, 2 * f)
                    for r0, picks in packed:
                        ins = dve.tensor_copy(idx_next[r0:r0 + rows, 0:picks.stop - picks.start], idx_f[R, picks])
                    ins.then_inc(idx_ready, 1)
                    assert count[0] == CHAIN, count

            with ExitStack() as inner:
                mx_tile = sb(inner, "mx_tile", [P, 2, KD, P])
                hx = sb(inner, "hx", [P, 2, D])
                hnn = sb(inner, "hnn", [P, 2, D])
                gf = sb(inner, "gf", [P, D])
                hst = [sb(inner, f"hst{i}", [P, 1]) for i in range(4)]
                pHH = ps(inner, "pHH", [P, 2, 1024])

                hx_in = [sem("hx_in0"), sem("hx_in1")]
                gf_in, mt_copied, h_mm, h_add = sem("gf_in"), sem("mt_copied"), sem("h_mm"), sem("h_add")
                h_sq, h_ms, h_sd, h_rs, h_norm = sem("h_sq"), sem("h_ms"), sem("h_sd"), sem("h_rs"), sem("h_norm")
                h_out = [sem("h_out0"), sem("h_out1")]

                def tiles():
                    ends = [0, 2, 5, 8, 10, 12, 14, 16, 16]
                    return [(t, t % 2, P if t < NT else TS, range(ends[max(t - 1, 0)], ends[t])) for t in range(NT + 1)]

                def hn_buf(t, par):
                    return hn_next if t == 0 else hnn[:, par]

                with nc.Block() as block:
                    @block.sync
                    def _(sp):
                        sp.dma_start(gf[:], norm_ffn_g.to_broadcast([P, D])).then_inc(gf_in, 16)
                        for t, par, rows, _ in tiles():
                            if t >= 2:
                                sp.wait_ge(h_out[par], 32 * (t // 2))
                            src = xp[t * P:(t + 1) * P, :] if rows == P else xs_dram
                            sp.dma_start(hx[0:rows, par, :], src).then_inc(hx_in[par], 16)
                            if t == 1:
                                keys = sub_keys[0].rearrange("h p n k -> n (h p) k")
                                for j in range(2):
                                    sp.dma_start(sk[j].rearrange("n (a k) -> n a k", k=P),
                                                 keys[:, j * NPC // 2:(j + 1) * NPC // 2, :]).then_inc(sk_in, 16)
                                for c in range(4):
                                    cols = slice(c * 4 * P, (c + 1) * 4 * P)
                                    sp.dma_start(wq[:, :, cols], w_query[0].rearrange("(c p) n -> p c n", p=P)[:, :, cols]
                                                 ).then_inc(wq_in[c], 16)

                    @block.gpsimd
                    def _(pool):
                        pool.iota(iota16[:], pattern=[[1, TOPK]], base=0, channel_multiplier=0,
                                  allow_small_or_imprecise_dtypes=True).then_inc(it_set, 1)
                        pool.wait_ge(it_set, 1)
                        for t, par, rows, _ in tiles():
                            if t >= 2:
                                pool.wait_ge(h_mm, t - 1)
                            pool.tensor_copy(mx_tile[:, par, :, 0:rows], mixedT[:, :, t * P:t * P + rows]
                                             ).then_inc(mt_copied, 1)
                            pool.wait_ge(mt_copied, t + 1)

                    @block.tensor
                    def _(pe):
                        pe.sem_inc(sc_done, 2)
                        for t, par, rows, pieces in tiles():
                            pe.wait_ge(mt_copied, t + 1)
                            if t >= 2:
                                pe.wait_ge(h_add, t - 1)
                            for half in range(2):
                                for c in range(KD):
                                    ins = pe.matmul(pHH[0:rows, par, half * 512:(half + 1) * 512],
                                                    mx_tile[:, par, c, 0:rows], wout[:, c, half * 512:(half + 1) * 512],
                                                    start=(c == 0), stop=(c == KD - 1))
                            ins.then_inc(h_mm, 1)
                            if t == 1:
                                pe.wait_ge(sk_in, 32)
                                for c in range(4):
                                    if c >= 2:
                                        pe.wait_ge(skT_copied, c - 1)
                                    for a in range(4):
                                        n = 4 * c + a
                                        ins = pe.transpose(pB[:, c % 2, a * P:(a + 1) * P],
                                                           sk[n // 8][:, (n % 8) * P:(n % 8 + 1) * P], ident[:])
                                    ins.then_inc(skT_done, 1)
                                pe.wait_ge(skT_copied, 4)
                                pe.wait_ge(h_norm, 1)
                            for g in pieces:
                                pe_choose(pe, 0, g, P, first=True)

                    @block.scalar
                    def _(act):
                        act.sem_inc(qT_copied, 2)
                        act.sem_inc(sc_copied, 2)
                        for t, par, rows, pieces in tiles():
                            hn = hn_buf(t, par)
                            act.wait_ge(h_add, t + 1)
                            if t >= 3:
                                act.wait_ge(h_out[par], 32 * (t // 2 - (1 - par)))
                            act.activation(hn[0:rows, :], hx[0:rows, par, :], ACT.Square,
                                           accum_out=hst[0][0:rows, :]).then_inc(h_sq, 1)
                            act.wait_ge(h_ms, t + 1)
                            act.activation(hst[2][0:rows, :], hst[1][0:rows, :], ACT.Sqrt).then_inc(h_sd, 1)
                            act.wait_ge(h_norm, t + 1)
                            row = slice(t * P, t * P + rows)
                            act.dma_start(h_dram[row, :], hx[0:rows, par, :]).then_inc(h_out[par], 16)
                            act.dma_start(hn_dram[row, :], hn[0:rows, :]).then_inc(h_out[par], 16)
                            if t == 1:
                                for c in range(4):
                                    act.wait_ge(skT_done, c + 1)
                                    act.activation(subT[:, 4 * c:4 * c + 4, :],
                                                   pB[:, c % 2, :].rearrange("p (a b) -> p a b", a=4),
                                                   ACT.Copy).then_inc(skT_copied, 1)
                            for g in pieces:
                                act_choose(act, 0, g, P)
                        act.wait_ge(h_out[0], 32 * (NT // 2 + 1))
                        act.wait_ge(h_out[1], 32 * (NT // 2))

                    @block.vector
                    def _(dve):
                        dve.sem_inc(sc_used, 2)
                        dve.wait_ge(gf_in, 16)
                        count = [0]
                        for t, par, rows, pieces in tiles():
                            dve.wait_ge(h_mm, t + 1)
                            dve.wait_ge(hx_in[par], 16 * (t // 2 + 1))
                            dve.tensor_tensor(hx[0:rows, par, :], pHH[0:rows, par, :], hx[0:rows, par, :],
                                              ALU.add).then_inc(h_add, 1)
                            dve.wait_ge(h_sq, t + 1)
                            dve.tensor_scalar(hst[1][0:rows, :], hst[0][0:rows, :], 1.0 / D, EPS, ALU.mult,
                                              ALU.add).then_inc(h_ms, 1)
                            dve.wait_ge(h_sd, t + 1)
                            dve.reciprocal(hst[3][0:rows, :], hst[2][0:rows, :]).then_inc(h_rs, 1)
                            dve.wait_ge(h_rs, t + 1)
                            dve.scalar_tensor_tensor(hn_buf(t, par)[0:rows, :], hx[0:rows, par, :], hst[3][0:rows, :],
                                                     gf[0:rows, :], ALU.mult, ALU.mult).then_inc(h_norm, 1)
                            if t == 1:
                                dve.wait_ge(it_set, 1)
                            for g in pieces:
                                dve_choose(dve, 0, g, P, count, first=True)

            ubuf = work[:, 0:RING * D].rearrange("p (a n) -> p a n", a=RING)
            vbuf = work[:, RING * D:2 * RING * D].rearrange("p (a n) -> p a n", a=RING)
            yo = work[:, 2 * RING * D:]
            hn_cur = sb(ctx, "hn_cur", [P, D])
            h_cur = sb(ctx, "h_cur", [P, D])
            idx_cur = sb(ctx, "idx_cur", [P, NPICK], U32)
            gw_cur = sb(ctx, "gw_cur", [P, NPICK])
            dots = sb(ctx, "dots", [P, 2, RING])
            gel = sb(ctx, "gel", [P, 2, RING])
            wgt = sb(ctx, "wgt", [P, 2, RING])
            dg = sb(ctx, "dg", [P, RING, P])
            ident2 = sb(ctx, "ident2", [P, TS])
            pY = ps(ctx, "pY", [P, 2, 512])

            i2_set = sem("i2_set")
            u_in = [sem(f"u_in{s}") for s in range(RING)]
            v_in = [sem(f"v_in{s}") for s in range(RING)]
            u_used, v_used = sem("u_used"), sem("v_used")
            gelu_done, w_done, dg_done = sem("gelu_done"), sem("w_done"), sem("dg_done")
            h_in, h_used, y_copied, y_out = sem("h_in"), sem("h_used"), sem("y_copied"), sem("y_out")

            with nc.Block() as block:
                @block.sync
                def _(sp):
                    def load_h(t, rows):
                        sp.dma_start(h_cur[0:rows, :], h_dram[ds(t * P, rows), :]).then_inc(h_in, 16)

                    def tile(t, rows, next_rows):
                        if next_rows:
                            sp.wait_ge(hn_moved, t + 1)
                            src = hn_dram[ds(t * P + P, next_rows), :]
                            sp.dma_start(hn_next[0:next_rows, :], src).then_inc(hn_in, 16)
                            if next_rows == TS:
                                sp.dma_start(hn_next[TS:P, :], src).then_inc(hn_in, 16)
                            sp.wait_ge(h_used, t + 1)
                            load_h(t + 1, next_rows)
                        sp.wait_ge(y_copied, t + 2)
                        dst = yp_out[ds(t * P, P), :] if rows == P else ys_out
                        sp.dma_start(dst, yo[0:rows, :]).then_inc(y_out, 16)
                    sp.sem_inc(y_out, 16)
                    sp.sem_inc(hn_in, 16)
                    load_h(0, P)
                    with sp.Fori(0, NT - 1) as t:
                        tile(t, P, P)
                    tile(NT - 1, P, TS)
                    tile(NT, TS, 0)
                    sp.wait_ge(y_out, 16 * (NT + 2))

                @block.gpsimd
                def _(pool):
                    def gather(t, k, buf, table, landed, used):
                        s = k % RING
                        hold(pool, used, NPICK * t + k + RING + 2)
                        pool.indirect_dma_start(
                            out=buf[:, s, :], out_offset=None, in_=table[0],
                            in_offset=bass.IndirectOffsetOnAxis(ap=idx_cur[:, k:k + 1], axis=0),
                        ).then_inc(landed[s], 16)

                    def gather_u(t, k):
                        gather(t, k, ubuf, peer_u, u_in, u_used)

                    def gather_v(t, k):
                        gather(t, k, vbuf, peer_v, v_in, v_used)

                    def take_early(t):
                        pool.wait_ge(idx_ready, t + 1)
                        pool.wait_ge(u_used, NPICK * t + 1)
                        hold(pool, v_used, NPICK * t + 1)
                        pool.tensor_copy(idx_cur[:, 0:NPICK - AHEAD], idx_next[:, 0:NPICK - AHEAD]).then_inc(idx_moved, 1)
                        hold(pool, idx_moved, 2 * t + 1)

                    def take_late(t):
                        pool.wait_ge(u_used, NPICK * t + CR)
                        hold(pool, v_used, NPICK * t + CR)
                        pool.tensor_copy(idx_cur[:, NPICK - AHEAD:], idx_next[:, NPICK - AHEAD:]).then_inc(idx_moved, 1)
                        hold(pool, idx_moved, 2 * t + 2)

                    def tile(t, picks, more):
                        for g in range(1, picks // RING):
                            if g == 3 and picks == NPICK:
                                take_late(t)
                            for s in range(RING):
                                gather_u(t, g * RING + s)
                                gather_v(t, (g - 1) * RING + s)
                        if more:
                            take_early(t + 1)
                        for s in range(RING):
                            if more:
                                gather_u(t + 1, s)
                            gather_v(t, picks - RING + s)
                    take_early(0)
                    for s in range(RING):
                        gather_u(0, s)
                    with pool.Fori(0, NT) as t:
                        tile(t, NPICK, True)
                    tile(NT, HALF, False)

                @block.tensor
                def _(pe):
                    pe.sem_inc(v_used, CR)

                    def weigh(t, g, picks, rows):
                        for s in range(RING):
                            k = g * RING + s
                            pe.wait_ge(v_in[s], 16 * (NGP * t + g + 1))
                            pe.wait_ge(dg_done, NPICK * t + k + 1)
                            for half in range(2):
                                ins = pe.matmul(pY[0:rows, half, :], dg[:, s, 0:rows],
                                                vbuf[:, s, half * 512:(half + 1) * 512],
                                                start=False, stop=(k == picks - 1))
                            ins.then_inc(v_used, 1)

                    def tile(t, picks, rows, next_rows):
                        for g in range(picks // RING):
                            if g == 1:
                                pe.wait_ge(h_in, 16 * t + 16)
                                pe.wait_ge(y_copied, t + 1)
                                for half in range(2):
                                    ins = pe.matmul(pY[0:rows, half, :], ident[0:rows, 0:rows],
                                                    h_cur[0:rows, half * 512:(half + 1) * 512], start=True, stop=False)
                                ins.then_inc(h_used, 1)
                            if g:
                                weigh(t, g - 1, picks, rows)
                            if next_rows and 0 in PIECES.get(g, ()):
                                pe.wait_ge(hn_in, 16 * t + (32 if next_rows == P else 48))
                            for n in PIECES.get(g, ()) if next_rows else ():
                                pe_choose(pe, t + 1, n, next_rows)
                        weigh(t, picks // RING - 1, picks, rows)
                    with pe.Fori(0, NT - 1) as t:
                        tile(t, NPICK, P, P)
                    tile(NT - 1, NPICK, P, TS)
                    tile(NT, HALF, TS, 0)

                @block.scalar
                def _(act):
                    for e in range(2):
                        ins = act.activation(ident2[e * TS:(e + 1) * TS, :], ident[e * TS:(e + 1) * TS, e * TS:(e + 1) * TS],
                                             ACT.Copy)
                    ins.then_inc(i2_set, 1)
                    act.wait_ge(i2_set, 1)
                    act.sem_inc(y_copied, 1)

                    def diagonals(t, g, rows):
                        act.wait_ge(w_done, NGP * t + g + 1)
                        eye = ident if rows == P else ident2
                        for s in range(RING):
                            act.wait_ge(v_used, NPICK * t + g * RING + s + RING + 2)
                            act.activation(dg[:, s, 0:rows], eye[:, 0:rows], ACT.Copy,
                                           scale=wgt[:, g % 2, s:s + 1]).then_inc(dg_done, 1)

                    def tile(t, picks, rows, next_rows):
                        for g in range(picks // RING):
                            if g:
                                diagonals(t, g - 1, rows)
                            for n in PIECES.get(g, ()) if next_rows else ():
                                act_choose(act, t + 1, n, next_rows)
                            act.wait_ge(u_used, NPICK * t + (g + 1) * RING + CR)
                            act.activation(gel[:, g % 2, :], dots[:, g % 2, :], ACT.Gelu).then_inc(gelu_done, 1)
                        diagonals(t, picks // RING - 1, rows)
                        act.wait_ge(v_used, NPICK * t + picks + CR)
                        act.wait_ge(y_out, 16 * t + 16)
                        act.activation(yo[0:rows, :], pY[0:rows].rearrange("p a b -> p (a b)"),
                                       ACT.Copy).then_inc(y_copied, 1)
                    with act.Fori(0, NT - 1) as t:
                        tile(t, NPICK, P, P)
                    tile(NT - 1, NPICK, P, TS)
                    tile(NT, HALF, TS, 0)

                @block.vector
                def _(dve):
                    dve.sem_inc(u_used, CR)

                    def weights(t, g):
                        dve.wait_ge(gelu_done, NGP * t + g + 1)
                        dve.tensor_tensor(wgt[:, g % 2, :], gel[:, g % 2, :],
                                          gw_cur[:, g * RING:(g + 1) * RING], ALU.mult).then_inc(w_done, 1)

                    def tile(t, picks, next_rows):
                        count = [0]
                        dve.wait_ge(idx_ready, t + 1)
                        if picks == HALF:
                            dve.wait_ge(hn_in, 16 * t + 32)
                        dve.wait_ge(u_used, NPICK * t + CR)
                        dve.tensor_copy(hn_cur[:], hn_next[:]).then_inc(hn_moved, 1)
                        dve.tensor_copy(gw_cur[:, 0:picks], gw_next[:, 0:picks]).then_inc(gw_moved, 1)
                        dve.wait_ge(hn_moved, t + 1)
                        dve.wait_ge(gw_moved, t + 1)
                        for g in range(picks // RING):
                            for s in range(RING):
                                if g and s == 3:
                                    weights(t, g - 1)
                                dve.wait_ge(u_in[s], 16 * (NGP * t + g + 1))
                                dve.tensor_tensor_reduce(ubuf[:, s, :], ubuf[:, s, :], hn_cur[:], 1.0, 0.0,
                                                         ALU.mult, ALU.add, dots[:, g % 2, s:s + 1]).then_inc(u_used, 1)
                            for n in PIECES.get(g, ()) if next_rows else ():
                                dve_choose(dve, t + 1, n, next_rows, count)
                        weights(t, picks // RING - 1)
                        dve.wait_ge(w_done, NGP * t + picks // RING)
                    with dve.Fori(0, NT - 1) as t:
                        tile(t, NPICK, P)
                    tile(NT - 1, NPICK, TS)
                    tile(NT, HALF, 0)


_INS = ['x_prompt', 'x_sample', 'cache_k', 'cache_v', 'cache_logf', 'state_pool', 'page_table', 'norm_mix_g',
        'w_in', 'b_forget', 'q_norm_g', 'k_norm_g', 'pool_mix_w', 'pool_scale', 'w_branch_pool',
        'w_branch_attn', 'w_out', 'norm_ffn_g', 'w_query', 'sub_keys', 'peer_u', 'peer_v']


def kernel(**inputs):
    import numpy as _np
    import concourse.bacc as _bacc
    from concourse import mybir as _mybir
    from concourse.bass_utils import run_bass_kernel_spmd as _run

    arrays, args = {}, []
    nc = _bacc.Bacc("TRN2", target_bir_lowering=False, num_devices=1)
    for name in _INS:
        a = _np.ascontiguousarray(inputs[name])
        arrays[f"in_{name}_dram"] = a
        args.append(nc.dram_tensor(f"in_{name}_dram", a.shape, _mybir.dt.from_np(a.dtype), kind="ExternalInput").ap())
    x_prompt, x_sample = inputs['x_prompt'], inputs['x_sample']
    batch, seq = x_prompt.shape[:2]
    dec, dseq = x_sample.shape[:2]
    depth, _, _, heads, dim = inputs['cache_k'].shape
    hist, dpool = inputs['state_pool'].shape[2:]
    outs = [x_prompt.shape, x_sample.shape,
            (depth, batch, seq, heads, dim), (depth, batch, seq, heads, dim), (depth, batch, seq, heads),
            (depth, batch, hist, dpool),
            (depth, dec, dseq, heads, dim), (depth, dec, dseq, heads, dim), (depth, dec, dseq, heads),
            (depth, dec, hist, dpool)]
    for i, shape in enumerate(outs):
        args.append(nc.dram_tensor(f"out_{i}_dram", tuple(shape), _mybir.dt.float32, kind="ExternalOutput").ap())
    build(nc, *args)
    r = _run(nc, [arrays], core_ids=[0])
    return tuple(r.results[0][f"out_{i}_dram"] for i in range(len(outs)))
```
